# Optimizing a Trainium2 kernel written in Bass

```python
import math
import jax, jax.numpy as jnp
from jax import lax
import numpy as np

D_MODEL = 2048
BATCH = 1
SEQ = 256
DEPTH = 2

HEAD_DIM = 64
EPS = 1e-6
NEG = -1e30
A_WIDTH = D_MODEL // 2
A_BLOCKS = 16
A_BLOCK = A_WIDTH // A_BLOCKS
CONV_WIDTH = 4
RG_C = 8.0
B_HEADS = (D_MODEL // 2) // HEAD_DIM
B_WIDTH = B_HEADS * HEAD_DIM
DILATION_PAIRS = ((128, 1), (512, 4), (2048, 16))
EVEN_IN = 2 * A_WIDTH + 3 * B_WIDTH
EVEN_MIX = A_WIDTH + B_WIDTH
C_HEADS = D_MODEL // (2 * HEAD_DIM)
C_QK = HEAD_DIM
C_V = 2 * HEAD_DIM
ODD_IN = C_HEADS * (4 * C_QK + C_V)
ODD_MIX = C_HEADS * C_V
Q_BLOCK = 128
ROPE_THETA = 500000.0
ROT_DIM = HEAD_DIM // 4
D_FF = -(-8 * D_MODEL // (3 * 256)) * 256
N_EVEN = (DEPTH + 1) // 2
N_ODD = DEPTH // 2

kernel_name = "hybrid_rglru_dilated_diffattn_encoder"

def rms_norm(x, g):
    xf = x.astype(jnp.float32)
    y = xf * lax.rsqrt(jnp.mean(xf * xf, axis=-1, keepdims=True) + EPS)
    return (y * g.astype(jnp.float32)).astype(x.dtype)

def rope_tables(seq):
    pos = jnp.arange(seq, dtype=jnp.float32)
    inv = ROPE_THETA ** (-jnp.arange(0, ROT_DIM, 2, dtype=jnp.float32) / ROT_DIM)
    ang = pos[:, None] * inv[None, :]
    return jnp.cos(ang), jnp.sin(ang)

def apply_partial_rope(x, cos, sin):
    half = ROT_DIM // 2
    shp = (1, x.shape[1]) + (1,) * (x.ndim - 3) + (half,)
    c = cos.reshape(shp)
    s = sin.reshape(shp)
    x1 = x[..., :half].astype(jnp.float32)
    x2 = x[..., half:ROT_DIM].astype(jnp.float32)
    return jnp.concatenate([x1 * c - x2 * s, x2 * c + x1 * s,
                            x[..., ROT_DIM:].astype(jnp.float32)], axis=-1)

def _lin_combine(left, right):
    a_l, b_l = left
    a_r, b_r = right
    return a_l * a_r, a_r * b_l + b_r

def linear_scan(a, u, reverse):
    _, h = lax.associative_scan(_lin_combine, (a, u), reverse=reverse, axis=1)
    return h

def bidirectional_rglru(xc, w_r, b_r, w_i, b_i, lam):
    bsz, seq, _ = xc.shape
    xf = xc.astype(jnp.float32)
    xb = xf.reshape(bsz, seq, A_BLOCKS, A_BLOCK)
    r = jax.nn.sigmoid(jnp.einsum('bsne,dnef->dbsnf', xb, w_r.astype(jnp.float32)).reshape(2, bsz, seq, A_WIDTH)
                       + b_r.astype(jnp.float32)[:, None, None, :])
    i = jax.nn.sigmoid(jnp.einsum('bsne,dnef->dbsnf', xb, w_i.astype(jnp.float32)).reshape(2, bsz, seq, A_WIDTH)
                       + b_i.astype(jnp.float32)[:, None, None, :])
    log_a = -RG_C * r * jax.nn.softplus(-lam.astype(jnp.float32))[:, None, None, :]
    a = jnp.exp(log_a)
    u = jnp.sqrt(jnp.maximum(-jnp.expm1(2.0 * log_a), 0.0)) * (i * xf[None])
    h_fwd = linear_scan(a[0], u[0], reverse=False)
    h_bwd = linear_scan(a[1], u[1], reverse=True)
    return h_fwd + h_bwd

def dilated_branch(q, k, v, window, dilation):
    bsz, seq, nh, dh = q.shape
    half = window // (2 * dilation)
    blk = half
    L = seq // dilation
    nb = -(-L // blk)
    pad = nb * blk - L

    def by_residue(t):
        return t.reshape(bsz, L, dilation, nh, dh).transpose(0, 2, 1, 3, 4)

    def neighbours(t):
        tp = jnp.pad(t, ((0, 0), (0, 0), (blk, pad + blk), (0, 0), (0, 0)))
        tp = tp.reshape(bsz, dilation, nb + 2, blk, nh, dh)
        return jnp.concatenate([tp[:, :, :-2], tp[:, :, 1:-1], tp[:, :, 2:]], axis=3)

    qb = jnp.pad(by_residue(q), ((0, 0), (0, 0), (0, pad), (0, 0), (0, 0)))
    qb = qb.reshape(bsz, dilation, nb, blk, nh, dh)
    kb = neighbours(by_residue(k))
    vb = neighbours(by_residue(v))
    s = jnp.einsum('bdnqhe,bdnkhe->bdnhqk', qb, kb)
    rel = jnp.arange(3 * blk)[None, :] - blk - jnp.arange(blk)[:, None]
    band = jnp.abs(rel) <= half
    key_u = jnp.arange(nb)[:, None] * blk - blk + jnp.arange(3 * blk)[None, :]
    inrange = (key_u >= 0) & (key_u < L)
    valid = band[None, :, :] & inrange[:, None, :]
    s = jnp.where(valid[None, None, :, None, :, :], s, NEG)
    m = jnp.max(s, axis=-1, keepdims=True)
    p = jnp.exp(s - m)
    den = jnp.sum(p, axis=-1, keepdims=True)
    o = jnp.einsum('bdnhqk,bdnkhe->bdnqhe', p, vb) / den.transpose(0, 1, 2, 4, 3, 5)
    lse = (m + jnp.log(den))[..., 0].transpose(0, 1, 2, 4, 3)

    def back(t):
        t = t.reshape((bsz, dilation, nb * blk) + t.shape[4:])[:, :, :L]
        t = jnp.swapaxes(t, 1, 2)
        return t.reshape((bsz, seq) + t.shape[3:])

    return back(o), back(lse)

def dilated_mixture_attention(q, k, v):
    outs, lses = [], []
    for window, dilation in DILATION_PAIRS:
        o, l = dilated_branch(q, k, v, window, dilation)
        outs.append(o)
        lses.append(l)
    wts = jax.nn.softmax(jnp.stack(lses, axis=0), axis=0)
    return jnp.sum(wts[..., None] * jnp.stack(outs, axis=0), axis=0)

def even_mixer(h, w_in, conv_w, conv_b, w_r, b_r, w_i, b_i, lam, w_out, cos, sin):
    bsz, seq, _ = h.shape
    z = h @ w_in
    o1, o2, o3, o4 = A_WIDTH, 2 * A_WIDTH, 2 * A_WIDTH + B_WIDTH, 2 * A_WIDTH + 2 * B_WIDTH
    gate, xr, q, k, v = z[..., :o1], z[..., o1:o2], z[..., o2:o3], z[..., o3:o4], z[..., o4:]
    xc = lax.conv_general_dilated(
        xr, conv_w[:, None, :], window_strides=(1,),
        padding=[(CONV_WIDTH // 2, CONV_WIDTH - 1 - CONV_WIDTH // 2)],
        dimension_numbers=('NWC', 'WIO', 'NWC'), feature_group_count=A_WIDTH) + conv_b
    y_a = bidirectional_rglru(xc, w_r, b_r, w_i, b_i, lam) * jax.nn.gelu(gate.astype(jnp.float32))
    q = apply_partial_rope(q.reshape(bsz, seq, B_HEADS, HEAD_DIM), cos, sin) * (HEAD_DIM ** -0.5)
    k = apply_partial_rope(k.reshape(bsz, seq, B_HEADS, HEAD_DIM), cos, sin)
    v = v.reshape(bsz, seq, B_HEADS, HEAD_DIM).astype(jnp.float32)
    y_b = dilated_mixture_attention(q, k, v).reshape(bsz, seq, B_WIDTH)
    y = jnp.concatenate([y_a, y_b], axis=-1).astype(w_out.dtype)
    return y @ w_out

def diff_attention_mixer(h, w_in, lq1, lk1, lq2, lk2, subln, w_out, lam_init, cos, sin):
    bsz, seq, _ = h.shape
    z = h @ w_in
    qk_w = C_HEADS * 2 * C_QK
    q = z[..., :qk_w].reshape(bsz, seq, C_HEADS, 2, C_QK)
    k = z[..., qk_w:2 * qk_w].reshape(bsz, seq, C_HEADS, 2, C_QK)
    v = z[..., 2 * qk_w:].reshape(bsz, seq, C_HEADS, C_V).astype(jnp.float32)
    q = apply_partial_rope(q, cos, sin) * (C_QK ** -0.5)
    k = apply_partial_rope(k, cos, sin)
    f32 = jnp.float32
    lam = (jnp.exp(jnp.sum(lq1.astype(f32) * lk1.astype(f32)))
           - jnp.exp(jnp.sum(lq2.astype(f32) * lk2.astype(f32))) + lam_init)
    nq = seq // Q_BLOCK
    qb = jnp.swapaxes(q.reshape(bsz, nq, Q_BLOCK, C_HEADS, 2, C_QK), 0, 1)

    def block(qblk):
        s = jnp.einsum('bqhje,bkhje->bhjqk', qblk, k)
        p = jax.nn.softmax(s, axis=-1)
        att = p[:, :, 0] - lam * p[:, :, 1]
        return jnp.einsum('bhqk,bkhe->bqhe', att, v)

    o = jnp.swapaxes(lax.map(block, qb), 0, 1).reshape(bsz, seq, C_HEADS, C_V)
    o = rms_norm(o, subln) * (1.0 - lam_init)
    return o.reshape(bsz, seq, ODD_MIX).astype(w_out.dtype) @ w_out

def swiglu(h, w_gate, w_up, w_down):
    return (jax.nn.silu(h @ w_gate) * (h @ w_up)) @ w_down

def setup_inputs(seed: int = 0) -> dict:
    key = jax.random.key(seed)
    ks = iter(jax.random.split(key, 40))

    def nrm(shape, scale):
        return jax.random.normal(next(ks), shape, jnp.float32) * scale

    def gain(shape):
        return 1.0 + nrm(shape, 0.02)

    x = nrm((BATCH, SEQ, D_MODEL), 1.0)
    norm_mix_pre = gain((DEPTH, D_MODEL))
    norm_mix_post = gain((DEPTH, D_MODEL))
    norm_ffn_pre = gain((DEPTH, D_MODEL))
    norm_ffn_post = gain((DEPTH, D_MODEL))
    ev_w_in = nrm((N_EVEN, D_MODEL, EVEN_IN), D_MODEL ** -0.5)
    ev_conv_w = nrm((N_EVEN, CONV_WIDTH, A_WIDTH), CONV_WIDTH ** -0.5)
    ev_conv_b = nrm((N_EVEN, A_WIDTH), 0.02)
    ev_w_r = nrm((N_EVEN, 2, A_BLOCKS, A_BLOCK, A_BLOCK), A_BLOCK ** -0.5)
    ev_b_r = nrm((N_EVEN, 2, A_WIDTH), 0.02)
    ev_w_i = nrm((N_EVEN, 2, A_BLOCKS, A_BLOCK, A_BLOCK), A_BLOCK ** -0.5)
    ev_b_i = nrm((N_EVEN, 2, A_WIDTH), 0.02)
    a_c = jax.random.uniform(next(ks), (N_EVEN, 2, A_WIDTH), jnp.float32, 0.9, 0.999)
    base = a_c ** (1.0 / RG_C)
    ev_lam = jnp.log(base) - jnp.log1p(-base)
    ev_w_out = nrm((N_EVEN, EVEN_MIX, D_MODEL), EVEN_MIX ** -0.5)
    od_w_in = nrm((N_ODD, D_MODEL, ODD_IN), D_MODEL ** -0.5)
    od_lam_q1 = nrm((N_ODD, C_QK), 0.1)
    od_lam_k1 = nrm((N_ODD, C_QK), 0.1)
    od_lam_q2 = nrm((N_ODD, C_QK), 0.1)
    od_lam_k2 = nrm((N_ODD, C_QK), 0.1)
    od_subln = gain((N_ODD, C_V))
    od_w_out = nrm((N_ODD, ODD_MIX, D_MODEL), ODD_MIX ** -0.5)
    ffn_w_gate = nrm((DEPTH, D_MODEL, D_FF), D_MODEL ** -0.5)
    ffn_w_up = nrm((DEPTH, D_MODEL, D_FF), D_MODEL ** -0.5)
    ffn_w_down = nrm((DEPTH, D_FF, D_MODEL), D_FF ** -0.5)
    return {"x": x, "norm_mix_pre": norm_mix_pre, "norm_mix_post": norm_mix_post,
            "norm_ffn_pre": norm_ffn_pre, "norm_ffn_post": norm_ffn_post,
            "ev_w_in": ev_w_in, "ev_conv_w": ev_conv_w, "ev_conv_b": ev_conv_b,
            "ev_w_r": ev_w_r, "ev_b_r": ev_b_r, "ev_w_i": ev_w_i, "ev_b_i": ev_b_i,
            "ev_lam": ev_lam, "ev_w_out": ev_w_out,
            "od_w_in": od_w_in, "od_lam_q1": od_lam_q1, "od_lam_k1": od_lam_k1,
            "od_lam_q2": od_lam_q2, "od_lam_k2": od_lam_k2, "od_subln": od_subln,
            "od_w_out": od_w_out,
            "ffn_w_gate": ffn_w_gate, "ffn_w_up": ffn_w_up, "ffn_w_down": ffn_w_down}

def reference(x, norm_mix_pre, norm_mix_post, norm_ffn_pre, norm_ffn_post,
              ev_w_in, ev_conv_w, ev_conv_b, ev_w_r, ev_b_r, ev_w_i, ev_b_i, ev_lam, ev_w_out,
              od_w_in, od_lam_q1, od_lam_k1, od_lam_q2, od_lam_k2, od_subln, od_w_out,
              ffn_w_gate, ffn_w_up, ffn_w_down):
    seq = x.shape[1]
    cos, sin = rope_tables(seq)
    for layer in range(DEPTH):
        h = rms_norm(x, norm_mix_pre[layer])
        j = layer // 2
        if layer % 2 == 0:
            m = even_mixer(h, ev_w_in[j], ev_conv_w[j], ev_conv_b[j], ev_w_r[j], ev_b_r[j],
                           ev_w_i[j], ev_b_i[j], ev_lam[j], ev_w_out[j], cos, sin)
        else:
            lam_init = 0.8 - 0.6 * math.exp(-0.3 * layer)
            m = diff_attention_mixer(h, od_w_in[j], od_lam_q1[j], od_lam_k1[j], od_lam_q2[j],
                                     od_lam_k2[j], od_subln[j], od_w_out[j], lam_init, cos, sin)
        x = x + rms_norm(m.astype(x.dtype), norm_mix_post[layer])
        h = rms_norm(x, norm_ffn_pre[layer])
        f = swiglu(h, ffn_w_gate[layer], ffn_w_up[layer], ffn_w_down[layer])
        x = x + rms_norm(f.astype(x.dtype), norm_ffn_post[layer])
    return x


_drawn_inputs = setup_inputs


def setup_inputs(seed=0):
    import zlib

    import numpy as np

    out = dict(_drawn_inputs(seed))
    spreads = {}
    factors = {'norm_ffn_post': 3.466,
     'ev_b_r': 8.0,
     'ev_b_i': 8.0,
     'od_lam_k2': 3.777,
     'od_subln': 40.896,
     'od_lam_k1': 3.431}
    for name, (base, spread) in spreads.items():
        noise = np.random.default_rng([zlib.crc32(name.encode()), seed]).standard_normal(out[name].shape)
        drawn = base * np.exp(spread * noise) if base else spread * noise
        out[name] = __import__('jax').numpy.asarray(drawn.astype(out[name].dtype))
    for name, factor in factors.items():
        out[name] = (out[name] * factor).astype(out[name].dtype)
    return out
```

```python
import math
from contextlib import ExitStack

import numpy as np

import concourse.bass as bass
from concourse import mybir

F32 = mybir.dt.float32
F32R = mybir.dt.float32r
BF16 = mybir.dt.bfloat16
ALU = mybir.AluOpType
ACT = mybir.ActivationFunctionType
AX = mybir.AxisListType

P = 128
T = 256
NT = T // P
D = 2048
KC = 512
KT = KC // P
NC = D // KC
EPS = 1e-6
NEG = -1e30
HD = 64
SCALE = HD ** -0.5
ROT = HD // 4
AW = D // 2
AT = AW // P
CONV = 4
DFF = -(-8 * D // (3 * 256)) * 256
NF = DFF // KC
CV = 2 * HD
LAM_INIT = 0.8 - 0.6 * math.exp(-0.3)
SCRATCH = 1024
RAW, HI, LO = 3, 4, 3
HI_LEAD, LO_LEAD = 3, 2
XP = T + CONV - 1
PAR = 3 * 2 * AT + (CONV + 1) * AT
C_LAM, C_BR, C_BI, C_CW, C_CB = 0, 2 * AT, 4 * AT, 6 * AT, 6 * AT + CONV * AT
HEADS_OF_GROUP = 8
SERIES = 9


class Task:

    def __init__(self, kind, b=0, layer=None, src=None, what=None, g=0, t=0, c=0, cb=0, i=0, n=0, u=0, s=0,
                 head=0, head_free=0, v_group=0, start=False, final=False, over_recurrence=False, evac=None):
        self.kind, self.b, self.layer = kind, b, layer
        self.src, self.what = src, what
        self.g, self.t, self.c, self.cb, self.i = g, t, c, cb, i
        self.n, self.u, self.s = n, u, s
        self.head, self.head_free, self.v_group = head, head_free, v_group
        self.start, self.final, self.over_recurrence, self.evac = start, final, over_recurrence, evac
        self.rope = 0
        self.e = self.m = self.prev_pt = self.tok_free = self.stage_free = None


class Slot:

    def __init__(self, u, kg, n, first, last, w=None, cb=0, region="h", recurrent=False):
        self.u, self.n, self.first, self.last = u, n, first, last
        self.w, self.kg, self.cb, self.lhs, self.recurrent = w, kg, cb, (region, kg), recurrent
        self.pre, self.post, self.events = [], [], None


class Body:

    def __init__(self, u, n, e, m, prev_gate):
        self.u, self.n, self.e, self.m, self.prev_gate, self.prev_up = u, n, e, m, prev_gate, prev_gate + 1


class Part:

    def __init__(self, kind, layer, slots=None):
        self.kind, self.layer, self.slots, self.b = kind, layer, slots, 2 * layer + (kind == "ffn")
        self.head = self.peeled = self.loop = self.tail = None
        self.tok_free = self.stage_free = self.n_gate = self.n_up = None


class Plan:

    def __init__(self):
        self.u = self.n = self.e = self.m = self.heads = self.ropes = 0
        self.ready, self.read, self.pt, self.parts = {}, {}, {}, []


def mixer_slots(plan, layer):
    slots, evacs, b = [], {}, 2 * layer

    def unit(w, kg, cb, region, first, last):
        slots.append(Slot(plan.u, kg, plan.n, first, last, w, cb, region, layer == 0 and region == "y" and kg < 2))
        plan.u += 1
        plan.n += last

    if layer == 0:
        order = ([("gate", g, g) for g in range(2)] + [("xr", g, 2 + g) for g in range(2)]
                 + [(w, g, 4 + 2 * i + g) for g in range(2) for i, w in enumerate("qkv")])
        groups, w_in, w_out = 2, "ev_in", "ev_out"
    else:
        order = [(w, g, 4 * i + g) for g in range(4) for i, w in enumerate("qkv")]
        groups, w_in, w_out = 4, "od_in", "od_out"

    def put(slot, front=False, **what):
        task = Task(layer=layer, b=b, **what)
        slots[slot].post.insert(0, task) if front else slots[slot].post.append(task)
        return task

    for what, g, cb in order:
        for kg in range(NC):
            unit(w_in, kg, cb, "h", kg == 0, kg == NC - 1)
        s = len(slots) - 1
        head_free = plan.heads + HEADS_OF_GROUP * (g - 1) if g >= 2 else 0
        evacs[what, g] = put(s, kind="evac", what=what, g=g, n=slots[s].n, u=slots[s].u, s=s, head_free=head_free)
        if what in ("q", "k"):
            evacs[what, g].rope = plan.ropes
            plan.ropes += NT
    n_in = len(slots)
    for kg in range(NC):
        for cb in range(NC):
            unit(w_out, kg, cb, "y", True, True)
            put(len(slots) - 1, kind="yadd", cb=cb, n=slots[-1].n, u=slots[-1].u, start=kg == 0, final=kg == NC - 1,
                over_recurrence=layer == 0 and kg == 0 and cb == 0)

    for (what, g), evac in evacs.items():
        if what != "v":
            for t in range(NT):
                put(evac.s + 1, kind="T", src=what, g=g, t=t, evac=evac)
    starts = [evacs["v", g].s + 1 + (layer == 0 and g == 0) for g in range(groups)]
    for s in range(len(slots)):
        for kind, lag in (("s0", 0), ("pt", 1), ("pv", 2), ("s", 0)):
            for g, start in enumerate(starts):
                i = s - start - lag
                if 0 <= i < HEADS_OF_GROUP:
                    put(s, kind=kind, g=g, i=i, n=plan.heads + HEADS_OF_GROUP * g + i, v_group=evacs["v", g].n)
    for g, start in enumerate(starts):
        kg = g + 2 if layer == 0 else g
        last_head = plan.heads + HEADS_OF_GROUP * (g + 1) - 1
        if layer == 1:
            put(start + HEADS_OF_GROUP + 1, kind="heads", g=g)
            put(start + HEADS_OF_GROUP + 2, kind="heads2", g=g)
        for t in range(NT):
            s = n_in if kg == 2 else start + HEADS_OF_GROUP + 2
            task = Task("T", b, layer, src="tok", g=kg, t=t, head=last_head)
            slots[s].post.insert(t if kg == 2 else len(slots[s].post), task)
    plan.heads += HEADS_OF_GROUP * groups
    if layer == 0:
        first = evacs["xr", 0].s + 3
        for i in range(AT):
            put(first + 2 * i - 1, front=True, kind="rg0", i=i)
            put(first + 2 * i, kind="rg1", i=i)
            put(first + 2 * i + 1, kind="rg2", i=i)
        for i in range(AT):
            put(first + 2 * i + 2, front=True, kind="rg3", i=i)
    add_boundary(slots, b)
    put(len(slots) - 1, kind="norm")
    slots[-1].post[-1].b = b + 1
    return slots


def add_boundary(slots, b):
    for c in range(NC):
        for c2 in ([0, 1] if c == 0 else [c + 1] if c + 1 < NC else []):
            for t in range(NT):
                slots[c].pre.append(Task("upd", b, c=c2, t=t))
        for t in range(NT):
            slots[c].pre.append(Task("T", b, src="x", g=c, t=t))
    slots[NC - 1].post.insert(0, Task("rsum", b))


def number_events(plan, tasks):
    for task in tasks:
        if task.kind == "T":
            task.e = plan.e
            plan.e += 1
            buffer = "tok" if task.src == "tok" or (task.src == "x" and task.g % 2 == 0) else "stage"
            plan.read[buffer, task.t] = task.e
            key = {"x": ("x", task.b), "tok": ("y", task.layer)}.get(task.src, (task.src, task.layer))
            plan.ready[(*key, task.g, task.t)] = task.e
            if task.src in ("x", "tok"):
                task.m = plan.m
                plan.m += 1
        elif task.kind == "pt":
            task.e = plan.e
            plan.e += 1
            plan.pt[task.n] = task.e
        elif task.kind in ("evac", "upd", "pv", "s"):
            task.tok_free = [plan.read.get(("tok", t)) for t in range(NT)]
            task.stage_free = [plan.read.get(("stage", t)) for t in range(NT)]
            if task.kind == "s":
                task.prev_pt = plan.pt.get(task.n - 1)


def make_plan():
    plan = Plan()
    for layer in range(2):
        slots = mixer_slots(plan, layer)
        for s in slots:
            number_events(plan, s.pre)
            number_events(plan, s.post)
        for s in slots:
            region, kg = s.lhs
            key = ("x", 2 * layer) if region == "h" else ("y", layer)
            s.events = None if s.recurrent else [plan.ready[(*key, kg, t)] for t in range(NT)]
        plan.parts.append(Part("mixer", layer, slots))
        f = Part("ffn", layer)
        f.head = [Slot(plan.u + i, i % NC, plan.n + i // NC, i % NC == 0, i % NC == NC - 1) for i in range(2 * NC)]
        add_boundary(f.head, f.b)
        for s in f.head:
            number_events(plan, s.pre)
        for s in f.head[:NC]:
            s.events = [plan.ready["x", f.b, s.kg, t] for t in range(NT)]
        f.tok_free = [plan.read["tok", t] for t in range(NT)]
        f.stage_free = [plan.read["stage", t] for t in range(NT)]
        n_gate, n_up = plan.n, plan.n + 1

        u1, n1 = plan.u + 2 * NC, plan.n + 2
        f.n_gate, f.n_up = n_gate, n_up
        f.peeled = Body(u1, n1, plan.e, plan.m, n_gate)
        f.loop = Body(u1 + 12, n1 + 6, plan.e + NT, plan.m + NT, n1)
        f.tail = Body(u1 + 12 * (NF - 1), n1 + 6 * (NF - 1), plan.e + NT * (NF - 1), plan.m + NT * (NF - 1),
                      n1 + 6 * (NF - 2))
        assert plan.e % 2 == 0 and plan.n % 2 == 0 and all(12 % ring == 0 for ring in (RAW, HI, LO))
        plan.u += 12 * NF
        plan.n += 6 * NF
        plan.e += NT * NF
        plan.m += NT * NF
        for t in range(NT):
            plan.read["tok", t] = plan.e - NT + t
        plan.parts.append(f)
    return plan


def trunk(nc, x, norm_mix_pre, norm_mix_post, norm_ffn_pre, norm_ffn_post,
          ev_w_in, ev_conv_w, ev_conv_b, ev_w_r, ev_b_r, ev_w_i, ev_b_i, ev_lam, ev_w_out,
          od_w_in, od_lam_q1, od_lam_k1, od_lam_q2, od_lam_k2, od_subln, od_w_out,
          ffn_w_gate, ffn_w_up, ffn_w_down, log_count, rope, identity, out):
    plan = make_plan()
    weights = {"ev_in": ev_w_in[0], "ev_out": ev_w_out[0], "od_in": od_w_in[0], "od_out": od_w_out[0]}
    x_rows = x[0].rearrange("(t p) d -> p t d", p=P)
    out_rows = out[0].rearrange("(t p) d -> p t d", p=P)

    with ExitStack() as ctx:
        def sb(name, shape, dt=F32):
            return ctx.enter_context(nc.sbuf_tensor(name, shape, dt))

        def sem(name):
            return ctx.enter_context(nc.semaphore(name))

        raw = [sb(f"raw{i}", [P, KT, KC]) for i in range(RAW)]
        w_hi = [sb(f"w_hi{i}", [P, KT, KC], F32R) for i in range(HI)]
        w_lo = [sb(f"w_lo{i}", [P, KT, KC], F32R) for i in range(LO)]
        xs = sb("xs", [P, NT, D])
        yacc = sb("yacc", [P, NT, D])
        h_hi = sb("h_hi", [P, D // P, T], F32R)
        h_lo = sb("h_lo", [P, D // P, T], F32R)
        y_hi = sb("y_hi", [P, 2 * KT, T], F32R)
        y_lo = sb("y_lo", [P, 2 * KT, T], F32R)
        tok = sb("tok", [P, NT, KC])
        stage = sb("stage", [P, NT, KC])
        gx = sb("gx", [P, max(AT * XP, D)])
        gq = sb("gq", [P, D])
        qT = [sb(f"qT{i}", [P, KT, T]) for i in range(2)]
        kT = [sb(f"kT{i}", [P, KT, T]) for i in range(2)]
        vb = [sb(f"vb{i}", [P, NT, KC]) for i in range(2)]
        prob = sb("prob", [P, 2, T])
        probT = sb("probT", [P, 2, T])
        logc = sb("logc", [P, NT, T])
        ropes = sb("ropes", [P, NT, 4 * (ROT // 2)])
        ident = sb("ident", [P, P])
        sub_gain = sb("sub_gain", [P, CV])
        junk = sb("junk", [P, KC], BF16)
        par = sb("par", [P, PAR])
        rot = sb("rot", [P, 2, KC // HD, ROT])
        lqk = rot[:, :, :, :].rearrange("p a b c -> p (a b c)")
        hc = sb("hc", [P, 2, 2 * AT])
        poly = sb("poly", [P, 4, 2 * AT])
        small = sb("small", [P, 72])

        pre_gain, post_gain = gx[:, 0:D], gq[:, :]
        xrT = gx[:, 0:AT * XP].rearrange("p (i t) -> p i t", i=AT)
        rg_w = [gq[:, 512 * i:512 * (i + 1)].rearrange("p (g f) -> p g f", g=4) for i in range(2)]
        rg_x = [gq[:, 1024 + T * i:1024 + T * (i + 1)] for i in range(2)]
        rg_h = gq[:, 1536:2048].rearrange("p (d t) -> p d t", d=2)
        flat = yacc[:, :, :].rearrange("p t d -> p (t d)")
        geluT = flat[:, 0:AT * T].rearrange("p (i t) -> p i t", i=AT)
        rg_r, rg_i, rg_a, rg_t = [flat[:, 2048 + 512 * i:2560 + 512 * i].rearrange("p (d t) -> p d t", d=2)
                                  for i in range(4)]
        ss_y, ss_x = small[:, 0:8].rearrange("p (t c) -> p t c", t=2), small[:, 8:16].rearrange("p (t c) -> p t c", t=2)
        var_y, var_x, rstd_y, rstd_x = small[:, 16:18], small[:, 18:20], small[:, 20:22], small[:, 22:24]
        mx, nmx = small[:, 24:26], small[:, 26:28]
        den = [small[:, 28 + 2 * i:30 + 2 * i] for i in range(2)]
        rden = small[:, 32:34]
        nlam, lam_e, lam_s = small[:, 34:35], small[:, 36:38], small[:, 38:40]
        sub_ss, sub_var, sub_r = small[:, 40:48], small[:, 48:56], small[:, 56:64]
        minus_half = small[:, 64:72]

        acc = [[ctx.enter_context(nc.psum_tensor(f"acc{i}{t}", [P, KC], F32)) for t in range(NT)] for i in range(2)]
        tp = [ctx.enter_context(nc.psum_tensor(f"tp{i}", [P, KT, P], F32)) for i in range(2)]
        sc = ctx.enter_context(nc.psum_tensor("sc", [P, 2, T], F32))
        pv = ctx.enter_context(nc.psum_tensor("pv", [P, 2, T], F32))

        landed = [sem(f"landed{i}") for i in range(RAW)]
        hi_done = sem("hi_done")
        lo_done = sem("lo_done")
        half_done = sem("half_done")
        unit_done = sem("unit_done")
        acc_free = [[sem(f"acc_free{i}{t}") for t in range(NT)] for i in range(2)]
        tp_done = sem("tp_done")
        tp_free = [sem(f"tp_free{i}") for i in range(2)]
        t_hi = sem("t_hi")
        x_in = sem("x_in")
        consts_in = sem("consts_in")
        par_in = sem("par_in")
        gain_in = [sem(f"gain_in{i}") for i in range(2)]
        rgw_in = [sem(f"rgw_in{i}") for i in range(2)]
        stored = sem("stored")
        sq_done = sem("sq_done")
        junk_done = sem("junk_done")
        var_done = sem("var_done")
        var_part = sem("var_part")
        rstd_done = sem("rstd_done")
        upd_part = sem("upd_part")
        upd_done = sem("upd_done")
        xg_done = sem("xg_done")
        rope_part = sem("rope_part")
        rope_done = sem("rope_done")
        s0_done = sem("s0_done")
        s_done = sem("s_done")
        max_part = sem("max_part")
        nmx_done = sem("nmx_done")
        s_free = sem("s_free")
        exp_done = sem("exp_done")
        att_part = sem("att_part")
        att_done = sem("att_done")
        pv_done = sem("pv_done")
        sub_sq = sem("sub_sq")
        sub_var_done = sem("sub_var_done")
        sub_rstd = sem("sub_rstd")
        heads_done = sem("heads_done")
        rden_done = sem("rden_done")
        o_done = sem("o_done")
        zero_done = sem("zero_done")
        par_T = sem("par_T")
        par_sb = sem("par_sb")
        prep_a = sem("prep_a")
        prep_v = sem("prep_v")
        conv_part = sem("conv_part")
        conv_done = sem("conv_done")
        gates_done = sem("gates_done")
        rg_act = sem("rg_act")
        rg_dve = sem("rg_dve")
        rg_sum = sem("rg_sum")
        rg_hi = sem("rg_hi")

        RG_ACT, RG_DVE, PREP = 9, 9, 25
        block = ctx.enter_context(nc.Block())

        def wait_event(eng, e):
            eng.wait_ge(tp_free[e % 2], e // 2 + 1)

        def wait_acc(eng, n, t):
            eng.wait_ge(acc_free[n % 2][t], n // 2 + 1)

        def wait_product(eng, u, t, off=0):
            eng.wait_ge(unit_done if t else half_done, u + 1 + off)

        def operand(lhs, hi, k, t):
            region, kg = lhs
            if region == "y" and kg < 2:
                src = y_hi if hi else y_lo
            else:
                src, kg = (h_hi if hi else h_lo), kg - 2 * (region == "y")
            return src[:, kg * KT + k, t * P:(t + 1) * P]

        def region_of(task):
            t = task.t
            if task.src == "x" or task.g >= 2:
                kt = KT * (task.g if task.src == "x" else task.g - 2)
                return [b[:, kt:kt + KT, t * P:(t + 1) * P] for b in (h_hi, h_lo)]
            return [b[:, KT * task.g:KT * (task.g + 1), t * P:(t + 1) * P] for b in (y_hi, y_lo)]

        def x_buffer(c):
            return tok if c % 2 == 0 else stage

        @block.sync
        def _(sp):
            def load(u, src, it=0):
                if u >= RAW:
                    sp.wait_ge(lo_done, u - RAW + 1 + 12 * it)
                sp.dma_start(raw[u % RAW][:, :, :], src.rearrange("(k p) n -> p k n", p=P)).then_inc(landed[u % RAW], 16)

            def gains(b):
                if b == 1:
                    sp.wait_ge(rg_dve, RG_DVE * AT)
                else:
                    sp.wait_ge(upd_done, 8 * (b - 1))
                    sp.wait_ge(xg_done, 8 * b)
                post = norm_mix_post[b // 2] if b % 2 else norm_ffn_post[b // 2 - 1]
                sp.dma_start(post_gain, post.partition_broadcast(P)).then_inc(gain_in[0], 16)
                if b < 4:
                    pre = norm_ffn_pre[b // 2] if b % 2 else norm_mix_pre[b // 2]
                    sp.dma_start(pre_gain, pre.partition_broadcast(P)).then_inc(gain_in[1], 16)

            for part in plan.parts:
                if part.kind == "mixer":
                    for s, slot in enumerate(part.slots):
                        load(slot.u, weights[slot.w][slot.kg * KC:(slot.kg + 1) * KC, slot.cb * KC:(slot.cb + 1) * KC])
                        if s == len(part.slots) - 12:
                            gains(2 * part.layer + 1)
                    continue
                wg, wu, wd = (w[part.layer] for w in (ffn_w_gate, ffn_w_up, ffn_w_down))

                def body(base, block, cols, rows, it=0):
                    for i in range(2 * NC):
                        load(base.u + i, (wg if i < NC else wu)[(i % NC) * KC:(i % NC + 1) * KC, cols], it)
                    for cb in range(NC):
                        load(base.u + 2 * NC + cb, wd[rows, cb * KC:(cb + 1) * KC], it)

                for i, slot in enumerate(part.head):
                    load(slot.u, (wg if i < NC else wu)[slot.kg * KC:(slot.kg + 1) * KC, 0:KC])
                gains(part.b + 1)
                body(part.peeled, 1, slice(KC, 2 * KC), slice(0, KC))
                with sp.Fori(0, NF - 2) as it:
                    body(part.loop, it + 2, bass.ds(it * KC + 2 * KC, KC), bass.ds(it * KC + KC, KC), it)
                for cb in range(NC):
                    load(part.tail.u + cb, wd[(NF - 1) * KC:NF * KC, cb * KC:(cb + 1) * KC])
            for c in range(NC):
                sp.wait_ge(upd_done, 24 + 2 * c + 2)
                sp.dma_start(out_rows[:, :, c * KC:(c + 1) * KC], xs[:, :, c * KC:(c + 1) * KC]).then_inc(stored, 16)
            sp.wait_ge(stored, 16 * NC)

        @block.scalar
        def _(act):
            for c in range(NC):
                act.dma_start(xs[:, :, c * KC:(c + 1) * KC], x_rows[:, :, c * KC:(c + 1) * KC]).then_inc(x_in, 16)
                if c == 0:
                    act.dma_start(pre_gain, norm_mix_pre[0].partition_broadcast(P)).then_inc(consts_in, 16)
                    act.dma_start(ident[:, :], identity).then_inc(consts_in, 16)
            for row, src in ((C_LAM, ev_lam[0].rearrange("d (i p) -> (d i) p", p=P)),
                             (C_BR, ev_b_r[0].rearrange("d (i p) -> (d i) p", p=P)),
                             (C_BI, ev_b_i[0].rearrange("d (i p) -> (d i) p", p=P)),
                             (C_CW, ev_conv_w[0].rearrange("j (i p) -> (j i) p", p=P)),
                             (C_CB, ev_conv_b[0].rearrange("(i p) -> i p", p=P))):
                act.dma_start(stage[row:row + src.shape[0], 1, 0:P], src).then_inc(par_in, 16)
            for i, src in enumerate((od_lam_q1, od_lam_k1, od_lam_q2, od_lam_k2)):
                act.dma_start(rot[:, :, :, :].rearrange("p a b c -> p (a b c)")[:, HD * i:HD * (i + 1)],
                              src[0].partition_broadcast(P)).then_inc(par_in, 16)
            act.dma_start(sub_gain[:, :], od_subln[0].partition_broadcast(P)).then_inc(par_in, 16)
            act.dma_start(logc[:, :, :], log_count.rearrange("(t p) k -> p t k", p=P)).then_inc(par_in, 16)
            act.dma_start(ropes[:, :, :], rope.rearrange("(t p) k -> p t k", p=P)).then_inc(par_in, 16)

            def recurrence_weights(i):
                for j, w in enumerate((ev_w_r, ev_w_i)):
                    for half in range(2):
                        p0 = HD * half
                        act.dma_start(rg_w[i % 2][p0:p0 + HD, 2 * j:2 * j + 2, p0:p0 + HD],
                                      w[0, :, 2 * i + half].rearrange("d e f -> e d f")).then_inc(rgw_in[i % 2], 16)

            def hi(u, it=0):
                act.wait_ge(landed[u % RAW], 16 * (u // RAW + 1) + 16 * (12 // RAW) * it)
                if u >= HI:
                    act.wait_ge(unit_done, u - HI + 1 + 12 * it)
                act.activation(w_hi[u % HI][:, :, :], raw[u % RAW][:, :, :], ACT.Copy).then_inc(hi_done, 1)

            def square(i, data):
                if i:
                    act.wait_ge(sq_done, i)
                b, j = divmod(i, 8)
                return act.activation(junk[:, 0:data[0].shape[-1]], data[0], ACT.Square, accum_out=data[1])

            def square_x(task):
                i = 16 * task.b + 2 * task.c + task.t
                if task.b == 0:
                    act.wait_ge(x_in, 16 * NC)
                else:
                    act.wait_ge(upd_done, 8 * (task.b - 1) + 2 * task.c + task.t + 1)
                    act.wait_ge(var_done, 2 * task.b)
                square(i, (xs[:, task.t, task.c * KC:(task.c + 1) * KC], ss_x[:, task.t, task.c:task.c + 1])).then_inc(sq_done, 1)

            def square_y(b, cb, n, t):
                i = 16 * b - 8 + 2 * cb + t
                wait_acc(act, n, t)
                square(i, (yacc[:, t, cb * KC:(cb + 1) * KC], ss_y[:, t, cb:cb + 1])).then_inc(sq_done, 1)

            def operand_hi(task):
                act.wait_ge(tp_done, task.e + 1)
                act.activation(region_of(task)[0], tp[task.e % 2][:, :, :], ACT.Copy).then_inc(t_hi, 1)

            def evac(task):
                slot, n = task.n % 2, task.n
                for t in range(NT):
                    wait_product(act, task.u, t)
                    if t == 0:
                        act.wait_ge(rstd_done, 2 * task.b + 1)
                    if task.what == "v":
                        if task.head_free:
                            act.wait_ge(o_done, task.head_free)
                        dst = vb[task.g % 2][:, t, :]
                    else:
                        if task.stage_free[t] is not None:
                            act.wait_ge(tp_done, task.stage_free[t] + 1)
                        dst = stage[:, t, :]
                    func = ACT.Gelu_apprx_tanh if task.what == "gate" else ACT.Copy
                    act.activation(dst, acc[slot][t][:, :], func, scale=rstd_x[:, t:t + 1]).then_inc(acc_free[slot][t], 1)

            def transposed(task):
                if task.src in ("x", "tok"):
                    operand_hi(task)
                    return
                act.wait_ge(tp_done, task.e + 1)
                t0 = task.t * P
                if task.src == "gate":
                    dst = geluT[:, KT * task.g:KT * (task.g + 1), t0:t0 + P]
                elif task.src == "xr":
                    if task.g == 0 and task.t == 0:
                        act.wait_ge(xg_done, 8)
                    dst = xrT[:, KT * task.g:KT * (task.g + 1), CONV // 2 + t0:CONV // 2 + t0 + P]
                else:
                    if task.evac.head_free:
                        act.wait_ge(o_done, task.evac.head_free)
                    dst = (qT if task.src == "q" else kT)[task.g % 2][:, :, t0:t0 + P]
                act.activation(dst, tp[task.e % 2][:, :, :], ACT.Copy).then_inc(tp_free[task.e % 2], 1)

            def softmax(task):
                n = task.n
                act.wait_ge(nmx_done, n + 1)
                if n >= 2:
                    act.wait_ge(o_done, n - 1)
                if task.layer == 0:
                    for t in range(NT):
                        ins = act.activation(prob[:, t, :], prob[:, t, :], ACT.Exp, scale=SCALE, bias=nmx[:, t:t + 1],
                                             accum_out=den[n % 2][:, t:t + 1])
                    ins.then_inc(exp_done, 1)
                else:
                    act.wait_ge(tp_done, task.prev_pt + 1)
                    for m in range(2):
                        ins = act.activation(prob[:, m, :], sc[:, m, :], ACT.Exp, scale=SCALE, bias=nmx[:, m:m + 1],
                                             accum_out=den[n % 2][:, m:m + 1])
                    ins.then_inc(exp_done, 1)

            def prob_transposed(task):
                n = task.n
                act.wait_ge(tp_done, task.e + 1)
                if n:
                    act.wait_ge(pv_done, n)
                flat_tp = tp[task.e % 2][:, :, :].rearrange("p a b -> p (a b)")
                flat_pt = probT[:, :, :].rearrange("p a b -> p (a b)")
                cols = 2 * T if task.layer == 0 else T
                act.activation(flat_pt[:, 0:cols], flat_tp[:, 0:cols], ACT.Copy).then_inc(tp_free[task.e % 2], 1)

            def values(task):
                if task.layer == 1:
                    hd, t = task.i // 2, task.i % 2
                    act.wait_ge(o_done, task.n + 1)
                    if task.n > 16:
                        act.wait_ge(sub_sq, task.n - 16)
                    if task.i == 0 and task.g:
                        act.wait_ge(sub_var_done, task.g)
                    act.activation(probT[:, 1, 0:CV], tok[:, t, hd * CV:(hd + 1) * CV], ACT.Square,
                                   accum_out=sub_ss[:, task.i:task.i + 1]).then_inc(sub_sq, 1)

            def rg1(i):
                act.wait_ge(gates_done, i + 1)
                if i + 2 < AT:
                    recurrence_weights(i + 2)
                if i == 0:
                    act.wait_ge(prep_v, PREP)
                if i:
                    act.wait_ge(rg_dve, RG_DVE * i)
                k = RG_ACT * i
                for d in range(2):
                    col = AT * d + i
                    act.activation(rg_r[:, d, :], sc[:, d, :], ACT.Tanh, scale=0.5, bias=par[:, C_BR + col:C_BR + col + 1]).then_inc(rg_act, 1)
                    act.activation(rg_i[:, d, :], pv[:, d, :], ACT.Tanh, scale=0.5, bias=par[:, C_BI + col:C_BI + col + 1]).then_inc(rg_act, 1)
                act.wait_ge(rg_act, k + 4)
                for d in range(2):
                    col = AT * d + i
                    act.activation(rg_a[:, d, :], rg_r[:, d, :], ACT.Exp, scale=hc[:, 1, col:col + 1], bias=hc[:, 1, col:col + 1]).then_inc(rg_act, 1)
                    act.activation(rg_t[:, d, :], rg_r[:, d, :], ACT.Tanh, scale=hc[:, 0, col:col + 1], bias=hc[:, 0, col:col + 1]).then_inc(rg_act, 1)

            def rg2(i):
                act.wait_ge(rg_dve, RG_DVE * i + 2)
                act.activation(rg_t[:, :, :], rg_t[:, :, :], ACT.Sqrt).then_inc(rg_act, 1)

            def rg3(i):
                act.wait_ge(rg_dve, RG_DVE * i + 8)
                act.activation(y_hi[:, i, :], rg_r[:, 1, :], ACT.Copy).then_inc(rg_hi, 1)

            def task_of(task):
                if task.kind == "T":
                    transposed(task)
                elif task.kind == "upd":
                    if task.b < 4:
                        square_x(task)
                elif task.kind == "evac":
                    evac(task)
                elif task.kind == "yadd" and task.final:
                    for t in range(NT):
                        square_y(task.b + 1, task.cb, task.n, t)
                elif task.kind == "s":
                    softmax(task)
                elif task.kind == "pt":
                    prob_transposed(task)
                elif task.kind == "pv":
                    values(task)
                elif task.kind == "rg1":
                    rg1(task.i)
                elif task.kind == "rg2":
                    rg2(task.i)
                elif task.kind == "rg3":
                    rg3(task.i)

            def silu(n, u, free, it=0):
                for t in range(NT):
                    wait_product(act, u, t, 12 * it)
                    free(t)
                    act.activation(stage[:, t, :], acc[n % 2][t][:, :], ACT.Silu, scale=rstd_x[:, t:t + 1]).then_inc(acc_free[n % 2][t], 1)

            def block_hi(base, it=0):
                for t in range(NT):
                    act.wait_ge(tp_done, base.e + t + 1 + NT * it)
                    act.activation(y_hi[:, 0:KT, t * P:(t + 1) * P], tp[t][:, :, :], ACT.Copy).then_inc(t_hi, 1)

            def body(base, it=0):
                block_hi(base, it)
                for i in range(12):
                    hi(base.u + i + HI_LEAD, it)
                    if i == NC - 1:
                        silu(base.n, base.u + i, lambda t: act.wait_ge(acc_free[base.prev_up % 2][t], base.prev_up // 2 + 1 + 3 * it), it)

            act.wait_ge(zero_done, 3)
            for i in range(2):
                recurrence_weights(i)
            act.wait_ge(par_T, 1)
            act.activation(par[:, :], sc[:, :, :].rearrange("p a b -> p (a b)")[:, 0:PAR], ACT.Copy).then_inc(par_sb, 1)
            act.wait_ge(prep_v, 1)
            act.activation(poly[:, 0, :], poly[:, 1, :], ACT.Exp, scale=-1.0).then_inc(prep_a, 1)
            act.wait_ge(prep_v, 4)
            act.activation(lam_e, lam_s, ACT.Exp).then_inc(prep_a, 1)
            for u in range(HI_LEAD):
                hi(u)
            for part in plan.parts:
                if part.kind == "mixer":
                    for slot in part.slots:
                        for task in slot.pre:
                            task_of(task)
                        hi(slot.u + HI_LEAD)
                        for task in slot.post:
                            task_of(task)
                    continue
                for i, slot in enumerate(part.head):
                    for task in slot.pre:
                        task_of(task)
                    hi(slot.u + HI_LEAD)
                    if i == NC - 1:
                        act.wait_ge(rstd_done, 2 * part.b + 1)
                        silu(part.n_gate, slot.u, lambda t: act.wait_ge(tp_done, part.stage_free[t] + 1))
                body(part.peeled)
                with act.Fori(0, NF - 2) as it:
                    body(part.loop, it)
                block_hi(part.tail)
                for cb in range(NC):
                    if part.tail.u + cb + HI_LEAD < plan.u:
                        hi(part.tail.u + cb + HI_LEAD)
                    for t in range(NT):
                        square_y(part.b + 1, cb, part.tail.n + cb, t)

        @block.tensor
        def _(pe):
            def unit(u, n, lhs, first, last, it=0):
                pe.wait_ge(lo_done, u + 1 + 12 * it)
                hi_tile, lo_tile = w_hi[u % HI], w_lo[u % LO]
                for t in range(NT):
                    if first and n >= 2:
                        pe.wait_ge(acc_free[n % 2][t], n // 2 + 3 * it)
                    for k in range(KT):
                        for j, (a, w) in enumerate(((1, hi_tile), (1, lo_tile), (0, hi_tile))):
                            mm = pe.matmul(acc[n % 2][t][:, :], operand(lhs, a, k, t), w[:, k, :],
                                           start=first and k == 0 and j == 0, stop=last and k == KT - 1 and j == 2)
                    mm.then_inc(unit_done if t else half_done, 1)

            def transposes(e, pieces, off=0):
                if e >= 2:
                    pe.wait_ge(tp_free[e % 2], e // 2 + off)
                for dst, src in pieces:
                    ins = pe.transpose(dst, src, ident[:, :])
                ins.then_inc(tp_done, 1)

            def quarter(e, src, t):
                return [(tp[e % 2][:, k, :], src[:, t, k * P:(k + 1) * P]) for k in range(KT)]

            def task_of(task):
                if task.kind == "T":
                    if task.src == "x":
                        pe.wait_ge(xg_done, 8 * task.b + 2 * task.g + task.t + 1)
                        src = x_buffer(task.g)
                    elif task.src == "tok":
                        if task.layer == 0:
                            pe.wait_ge(o_done, task.head + 1)
                        else:
                            pe.wait_ge(heads_done, task.g + 1)
                        src = tok
                    else:
                        src = stage
                        if task.src in ("q", "k"):
                            pe.wait_ge(rope_done, task.evac.rope + task.t + 1)
                        else:
                            wait_acc(pe, task.evac.n, task.t)
                    transposes(task.e, quarter(task.e, src, task.t))
                elif task.kind == "rg1":
                    i = task.i
                    pe.wait_ge(conv_done, i + 1)
                    pe.wait_ge(rgw_in[i % 2], 64 * (i // 2 + 1))
                    if i == 0:
                        pe.wait_ge(par_sb, 1)
                    else:
                        pe.wait_ge(rg_act, RG_ACT * (i - 1) + 4)
                    for j, bank in enumerate((sc, pv)):
                        for d in range(2):
                            mm = pe.matmul(bank[:, d, :], rg_w[i % 2][:, 2 * j + d, :], rg_x[i % 2], start=True, stop=True)
                    mm.then_inc(gates_done, 1)
                elif task.kind in ("s0", "s"):
                    n, j = task.n, int(task.kind == "s")
                    if j:
                        pe.wait_ge(s0_done, n + 1)
                    elif n > 16:
                        pe.wait_ge(exp_done, n)
                    elif n:
                        pe.wait_ge(s_free, n)
                    else:
                        pe.wait_ge(rg_act, RG_ACT * (AT - 1) + 4)
                    if task.i == 0:
                        for src in "qk":
                            for t in range(NT):
                                wait_event(pe, plan.ready[src, task.layer, task.g, t])
                    q, k = qT[task.g % 2], kT[task.g % 2]
                    if task.layer == 0:
                        r, kt, t = HD * (task.i % 2), task.i // 2, j
                    else:
                        r, kt, t = HD * j, task.i // 2, task.i % 2
                    pe.matmul(sc[:, j, :], q[r:r + HD, kt, t * P:(t + 1) * P], k[r:r + HD, kt, :],
                              start=True, stop=True).then_inc(s_done if j else s0_done, 1)
                elif task.kind == "pt":
                    if task.layer == 0:
                        pe.wait_ge(exp_done, task.n + 1)
                        flat_tp = tp[task.e % 2][:, :, :].rearrange("p a b -> p (a b)")
                        transposes(task.e, [(flat_tp[:, j * T + t * P:j * T + (t + 1) * P], prob[:, t, j * P:(j + 1) * P])
                                            for j in range(2) for t in range(NT)])
                    else:
                        pe.wait_ge(att_done, task.n - 16 + 1)
                        transposes(task.e, [(tp[task.e % 2][:, j, :], prob[:, 0, j * P:(j + 1) * P]) for j in range(2)])
                elif task.kind == "pv":
                    n = task.n
                    wait_event(pe, plan.pt[n])
                    if n:
                        pe.wait_ge(o_done, n)
                    if task.i == 0:
                        for t in range(NT):
                            wait_acc(pe, task.v_group, t)
                    v = vb[task.g % 2]
                    if task.layer == 0:
                        for t in range(NT):
                            for j in range(2):
                                mm = pe.matmul(pv[:, 0, t * HD:(t + 1) * HD], probT[:, j, t * P:(t + 1) * P],
                                               v[:, j, task.i * HD:(task.i + 1) * HD], start=j == 0, stop=j == 1)
                    else:
                        flat_pt, hd = probT[:, 0, :], task.i // 2
                        for j in range(2):
                            mm = pe.matmul(pv[:, 0, 0:CV], flat_pt[:, j * P:(j + 1) * P], v[:, j, hd * CV:(hd + 1) * CV],
                                           start=j == 0, stop=j == 1)
                    mm.then_inc(pv_done, 1)

            def operand_ready(slot):
                if slot.recurrent:
                    pe.wait_ge(rg_dve, RG_DVE * KT * (slot.kg + 1))
                else:
                    for t in range(NT):
                        wait_event(pe, slot.events[t])

            pe.wait_ge(par_in, 16 * 12)
            pe.wait_ge(consts_in, 32)
            pe.transpose(sc[:, :, :].rearrange("p a b -> p (a b)")[:, 0:PAR], stage[0:PAR, 1, 0:P], ident[0:PAR, 0:PAR]).then_inc(par_T, 1)
            for part in plan.parts:
                if part.kind == "mixer":
                    for slot in part.slots:
                        for task in slot.pre:
                            task_of(task)
                        operand_ready(slot)
                        unit(slot.u, slot.n, slot.lhs, slot.first, slot.last)
                        for task in slot.post:
                            task_of(task)
                    continue
                for i, slot in enumerate(part.head):
                    for task in slot.pre:
                        task_of(task)
                    if i < NC:
                        operand_ready(slot)
                    unit(slot.u, slot.n, ("h", slot.kg), slot.first, slot.last)

                def down_operand(base, it=0):
                    for t in range(NT):
                        pe.wait_ge(acc_free[base.prev_up % 2][t], base.prev_up // 2 + 1 + 3 * it)
                        transposes(base.e + t, quarter(base.e + t, tok, t), off=it)

                def down(u, n, base, it=0):
                    for t in range(NT):
                        pe.wait_ge(tp_free[t], base.e // 2 + 1 + it)
                    for cb in range(NC):
                        unit(u + cb, n + cb, ("y", 0), True, True, it)

                def body(base, it=0):
                    down_operand(base, it)
                    for i in range(2 * NC):
                        unit(base.u + i, base.n + i // NC, ("h", i % NC), i % NC == 0, i % NC == NC - 1, it)
                    down(base.u + 2 * NC, base.n + 2, base, it)

                body(part.peeled)
                with pe.Fori(0, NF - 2) as it:
                    body(part.loop, it)
                down_operand(part.tail)
                down(part.tail.u, part.tail.n, part.tail)

        @block.vector
        def _(dve):
            def lo(u, it=0):
                dve.wait_ge(hi_done, u + 1 + 12 * it)
                if u >= LO:
                    dve.wait_ge(unit_done, u - LO + 1 + 12 * it)
                dve.tensor_tensor(w_lo[u % LO][:, :, :], raw[u % RAW][:, :, :],
                                  w_hi[u % HI][:, :, :].bitcast(F32), ALU.subtract).then_inc(lo_done, 1)

            def operand_lo(e, m, hi_ap, lo_ap, it=0):
                dve.wait_ge(t_hi, m + 1 + NT * it)
                dve.tensor_tensor(lo_ap, tp[e % 2][:, :, :], hi_ap.bitcast(F32), ALU.subtract).then_inc(tp_free[e % 2], 1)

            def mean(b, which, sums, var, squares):
                k = 2 * b + which
                dve.wait_ge(sq_done, squares)
                if k:
                    dve.wait_ge(rstd_done, k)
                dve.tensor_reduce(var, sums, AX.X, ALU.add).then_inc(var_part, 1)
                dve.wait_ge(var_part, k + 1)
                dve.tensor_scalar(var, var, 1.0 / D, EPS, ALU.mult, ALU.add).then_inc(var_done, 1)

            def update(task):
                if task.b == 0:
                    return
                k = 8 * (task.b - 1) + 2 * task.c + task.t
                if task.c == 0:
                    dve.wait_ge(rstd_done, 2 * task.b)
                    dve.wait_ge(gain_in[0], 16 * task.b)
                cols = slice(task.c * KC, (task.c + 1) * KC)
                y, r = yacc[:, task.t, cols], xs[:, task.t, cols]
                dve.scalar_tensor_tensor(y, y, rstd_y[:, task.t:task.t + 1], post_gain[:, cols], ALU.mult, ALU.mult).then_inc(upd_part, 1)
                dve.wait_ge(upd_part, k + 1)
                dve.tensor_tensor(r, y, r, ALU.add).then_inc(upd_done, 1)

            def yadd(n, u, cb, start, it=0):
                for t in range(NT):
                    wait_product(dve, u, t, 12 * it)
                    y, a = yacc[:, t, cb * KC:(cb + 1) * KC], acc[n % 2][t][:, :]
                    if start:
                        dve.tensor_copy(y, a).then_inc(acc_free[n % 2][t], 1)
                    else:
                        dve.tensor_tensor(y, a, y, ALU.add).then_inc(acc_free[n % 2][t], 1)

            def softmax(task):
                n = task.n
                dve.wait_ge(s_done, n + 1)
                if n:
                    dve.wait_ge(exp_done, n)
                if task.layer == 0:
                    if n:
                        dve.wait_ge(tp_done, task.prev_pt + 1)
                    for t in range(NT):
                        ins = dve.tensor_tensor_reduce(prob[:, t, :], sc[:, t, :], logc[:, t, :], 1.0, 3.0 * NEG,
                                                       ALU.add, ALU.max, mx[:, t:t + 1])
                    ins.then_inc(s_free, 1)
                    dve.wait_ge(s_free, n + 1)
                else:
                    dve.tensor_reduce(mx, sc[:, :, :], AX.X, ALU.max).then_inc(max_part, 1)
                    dve.wait_ge(max_part, n - 16 + 1)
                dve.tensor_scalar(nmx, mx, -SCALE, None, ALU.mult).then_inc(nmx_done, 1)

            def difference(task):
                n, k = task.n, 3 * (task.n - 16)
                dve.wait_ge(exp_done, n + 1)
                if k:
                    dve.wait_ge(att_done, n - 16)
                dve.reciprocal(rden, den[n % 2]).then_inc(att_part, 1)
                dve.wait_ge(att_part, k + 1)
                dve.tensor_tensor(rden[:, 1:2], rden[:, 1:2], nlam, ALU.mult).then_inc(att_part, 1)
                dve.tensor_scalar(prob[:, 0, :], prob[:, 0, :], rden[:, 0:1], None, ALU.mult).then_inc(att_part, 1)
                dve.wait_ge(att_part, k + 3)
                dve.scalar_tensor_tensor(prob[:, 0, :], prob[:, 1, :], rden[:, 1:2], prob[:, 0, :], ALU.mult, ALU.add).then_inc(att_done, 1)

            def values(task):
                n = task.n
                dve.wait_ge(pv_done, n + 1)
                for t in range(NT):
                    if task.i == 0 and task.tok_free[t] is not None:
                        dve.wait_ge(tp_done, task.tok_free[t] + 1)
                if task.layer == 0:
                    if n:
                        dve.wait_ge(o_done, n)
                    dve.reciprocal(rden, den[n % 2]).then_inc(rden_done, 1)
                    dve.wait_ge(rden_done, n + 1)
                    for t in range(NT):
                        ins = dve.tensor_scalar(tok[:, t, task.i * HD:(task.i + 1) * HD], pv[:, 0, t * HD:(t + 1) * HD],
                                                rden[:, t:t + 1], None, ALU.mult)
                    ins.then_inc(o_done, 1)
                else:
                    hd, t = task.i // 2, task.i % 2
                    dve.tensor_copy(tok[:, t, hd * CV:(hd + 1) * CV], pv[:, 0, 0:CV]).then_inc(o_done, 1)

            def heads_mean(g):
                dve.wait_ge(sub_sq, HEADS_OF_GROUP * (g + 1))
                if g:
                    dve.wait_ge(sub_rstd, g)
                dve.tensor_scalar(sub_var, sub_ss, 1.0 / CV, EPS, ALU.mult, ALU.add).then_inc(sub_var_done, 1)

            def heads_scale(g):
                dve.wait_ge(sub_rstd, g + 1)
                for i in range(HEADS_OF_GROUP):
                    o = tok[:, i % 2, i // 2 * CV:(i // 2 + 1) * CV]
                    ins = dve.scalar_tensor_tensor(o, o, sub_r[:, i:i + 1], sub_gain[:, :], ALU.mult, ALU.mult)
                ins.then_inc(heads_done, 1)

            def rg1(i):
                k = RG_DVE * i
                dve.wait_ge(rg_act, RG_ACT * i + 8)
                dve.tensor_tensor(rg_r[:, :, :], rg_a[:, :, :], rg_a[:, :, :], ALU.mult).then_inc(rg_dve, 1)
                dve.wait_ge(rg_dve, k + 1)
                dve.scalar_tensor_tensor(rg_t[:, :, :], rg_r[:, :, :], 1.0, rg_t[:, :, :], ALU.add, ALU.mult).then_inc(rg_dve, 1)

            def rg2(i):
                k = RG_DVE * i
                for d in range(2):
                    dve.scalar_tensor_tensor(rg_i[:, d, :], rg_i[:, d, :], 1.0, rg_x[i % 2], ALU.add, ALU.mult).then_inc(rg_dve, 1)
                dve.wait_ge(rg_dve, k + 4)
                dve.wait_ge(rg_act, RG_ACT * i + 9)
                dve.scalar_tensor_tensor(rg_i[:, :, :], rg_i[:, :, :], 0.5, rg_t[:, :, :], ALU.mult, ALU.mult).then_inc(rg_dve, 1)
                dve.wait_ge(rg_dve, k + 5)
                dve.tensor_tensor_scan(rg_h[:, 0, :], rg_a[:, 0, :], rg_i[:, 0, :], 0.0, ALU.mult, ALU.add).then_inc(rg_dve, 1)
                dve.tensor_tensor_scan(rg_h[:, 1, ::-1], rg_a[:, 1, ::-1], rg_i[:, 1, ::-1], 0.0, ALU.mult, ALU.add).then_inc(rg_dve, 1)

            def rg3(i):
                k = RG_DVE * i
                dve.wait_ge(rg_sum, i + 1)
                dve.tensor_tensor(rg_r[:, 1, :], rg_r[:, 0, :], geluT[:, i, :], ALU.mult).then_inc(rg_dve, 1)
                dve.wait_ge(rg_hi, i + 1)
                dve.tensor_tensor(y_lo[:, i, :], rg_r[:, 1, :], y_hi[:, i, :].bitcast(F32), ALU.subtract).then_inc(rg_dve, 1)

            def task_of(task):
                if task.kind == "T":
                    if task.src in ("x", "tok"):
                        operand_lo(task.e, task.m, *region_of(task))
                elif task.kind == "upd":
                    update(task)
                elif task.kind == "rsum":
                    mean(task.b, 0, ss_x, var_x, 16 * task.b + 8)
                elif task.kind == "norm":
                    mean(task.b - 1, 1, ss_y, var_y, 16 * task.b)
                elif task.kind == "yadd":
                    if task.over_recurrence:
                        dve.wait_ge(rg_dve, RG_DVE * AT)
                    yadd(task.n, task.u, task.cb, task.start)
                elif task.kind == "s":
                    softmax(task)
                elif task.kind == "heads":
                    heads_mean(task.g)
                elif task.kind == "pv":
                    values(task)
                elif task.kind == "rg1":
                    rg1(task.i)
                elif task.kind == "rg2":
                    rg2(task.i)
                elif task.kind == "rg3":
                    rg3(task.i)

            v = [0]

            def prep(ins):
                ins.then_inc(prep_v, 1)
                v[0] += 1
                dve.wait_ge(prep_v, v[0])

            lam = par[:, C_LAM:C_LAM + 2 * AT]
            dve.wait_ge(par_sb, 1)
            dve.wait_ge(par_in, 16 * 12)
            prep(dve.scalar_tensor_tensor(poly[:, 1, :], lam, -1.0, lam, ALU.mult, ALU.max))
            for i in range(2):
                prep(dve.tensor_tensor_reduce(prob[:, i, 0:HD], lqk[:, 2 * HD * i:2 * HD * i + HD],
                                              lqk[:, 2 * HD * i + HD:2 * HD * (i + 1)], 1.0, 0.0, ALU.mult, ALU.add,
                                              lam_s[:, i:i + 1]))
            prep(dve.tensor_scalar(sub_gain[:, :], sub_gain[:, :], 1.0 - LAM_INIT, None, ALU.mult))
            dve.wait_ge(prep_a, 1)
            e, s, z, q = poly[:, 0, :], poly[:, 1, :], poly[:, 2, :], poly[:, 3, :]
            prep(dve.tensor_scalar(s, e, 2.0, None, ALU.add))
            prep(dve.reciprocal(z, s))
            prep(dve.tensor_tensor(s, e, z, ALU.mult))
            prep(dve.tensor_tensor(z, s, s, ALU.mult))
            prep(dve.tensor_scalar(q, z, 1.0 / (2 * SERIES + 1), None, ALU.mult))
            for k in range(SERIES - 1, 0, -1):
                prep(dve.scalar_tensor_tensor(q, q, 1.0 / (2 * k + 1), z, ALU.add, ALU.mult))
            prep(dve.scalar_tensor_tensor(q, q, 1.0, s, ALU.add, ALU.mult))
            prep(dve.tensor_scalar(z, lam, -1.0, 0.0, ALU.mult, ALU.max))
            prep(dve.scalar_tensor_tensor(z, q, 2.0, z, ALU.mult, ALU.add))
            prep(dve.tensor_scalar(hc[:, 0, :], z, 4.0, None, ALU.mult))
            prep(dve.tensor_scalar(hc[:, 1, :], z, -4.0, None, ALU.mult))
            prep(dve.tensor_scalar(par[:, C_BR:C_CW], par[:, C_BR:C_CW], 0.5, None, ALU.mult))
            dve.wait_ge(prep_a, 2)
            prep(dve.tensor_tensor(nlam, lam_e[:, 1:2], lam_e[:, 0:1], ALU.subtract))
            prep(dve.tensor_scalar(nlam, nlam, LAM_INIT, None, ALU.subtract))
            for u in range(LO_LEAD):
                lo(u)
            for part in plan.parts:
                if part.kind == "mixer":
                    for slot in part.slots:
                        for task in slot.pre:
                            task_of(task)
                        for task in slot.post:
                            if task.kind == "pt" and task.layer == 1:
                                difference(task)
                            elif task.kind == "heads2":
                                heads_scale(task.g)
                        lo(slot.u + LO_LEAD)
                        for task in slot.post:
                            task_of(task)
                    continue

                def gate_up(n_gate, n_up, u, tok_free, it=0):
                    for t in range(NT):
                        wait_product(dve, u, t, 12 * it)
                        dve.wait_ge(acc_free[n_gate % 2][t], n_gate // 2 + 1 + 3 * it)
                        tok_free(t)
                        dve.scalar_tensor_tensor(tok[:, t, :], acc[n_up % 2][t][:, :], rstd_x[:, t:t + 1], stage[:, t, :],
                                                 ALU.mult, ALU.mult).then_inc(acc_free[n_up % 2][t], 1)

                def block_lo(base, it=0):
                    for t in range(NT):
                        operand_lo(base.e + t, base.m + t, y_hi[:, 0:KT, t * P:(t + 1) * P],
                                   y_lo[:, 0:KT, t * P:(t + 1) * P], it)

                def body(base, start, it=0):
                    block_lo(base, it)
                    for i in range(12):
                        lo(base.u + i + LO_LEAD, it)
                        if i == 2 * NC - 1:
                            gate_up(base.n, base.n + 1, base.u + i, lambda t: dve.wait_ge(tp_done, base.e + t + 1 + NT * it), it)
                        if i >= 2 * NC:
                            yadd(base.n + 2 + i - 2 * NC, base.u + i, i - 2 * NC, start, it)

                for i, slot in enumerate(part.head):
                    for task in slot.pre:
                        task_of(task)
                    lo(slot.u + LO_LEAD)
                    for task in slot.post:
                        task_of(task)
                gate_up(part.n_gate, part.n_up, part.head[-1].u, lambda t: dve.wait_ge(tp_done, part.tok_free[t] + 1))
                body(part.peeled, True)
                with dve.Fori(0, NF - 2) as it:
                    body(part.loop, False, it)
                block_lo(part.tail)
                for cb in range(NC):
                    if part.tail.u + cb + LO_LEAD < plan.u:
                        lo(part.tail.u + cb + LO_LEAD)
                    yadd(part.tail.n + cb, part.tail.u + cb, cb, False)
                mean(part.b, 1, ss_y, var_y, 16 * (part.b + 1))
            for c in range(NC):
                for t in range(NT):
                    update(Task("upd", 4, c=c, t=t))

        @block.gpsimd
        def _(pool):
            pool.memset(minus_half, -0.5).then_inc(zero_done, 1)
            for i in range(2):
                pool.memset(rg_w[i], 0.0).then_inc(zero_done, 1)
            pool.wait_ge(zero_done, 3)

            def rsqrt(k, dst, var):
                pool.wait_ge(var_done, k + 1)
                pool.tensor_tensor(dst, var, minus_half[:, 0:NT], ALU.pow).then_inc(rstd_done, 1)

            def gained(task):
                if task.b == 0:
                    pool.wait_ge(x_in, 16 * NC)
                    pool.wait_ge(consts_in, 32)
                    if task.c == 1 and task.t == 1:
                        pool.wait_ge(par_T, 1)
                else:
                    pool.wait_ge(upd_done, 8 * (task.b - 1) + 2 * task.c + task.t + 1)
                    pool.wait_ge(gain_in[1], 16 * task.b)
                last = (task.stage_free if task.c % 2 else task.tok_free)[task.t]
                if last is not None:
                    pool.wait_ge(tp_done, last + 1)
                cols = slice(task.c * KC, (task.c + 1) * KC)
                pool.tensor_tensor(x_buffer(task.c)[:, task.t, :], xs[:, task.t, cols], pre_gain[:, cols], ALU.mult).then_inc(xg_done, 1)

            def rotate(task):
                for t in range(NT):
                    k = 3 * (task.rope + t)
                    wait_acc(pool, task.n, t)
                    if task.rope + t:
                        pool.wait_ge(rope_done, task.rope + t)
                    else:
                        pool.wait_ge(par_in, 16 * 12)
                        pool.wait_ge(prep_v, 3)
                    heads = stage[:, t, :].rearrange("p (h e) -> p h e", e=HD)
                    h2 = ROT // 2
                    table = ropes[:, t, :].rearrange("p (o e) -> p o e", o=1)

                    def per_head(a, b):
                        return table[:, :, a:b].broadcast_to([P, KC // HD, b - a])
                    pool.tensor_tensor(rot[:, 0], heads[:, :, 0:ROT], per_head(0, ROT), ALU.mult).then_inc(rope_part, 1)
                    pool.tensor_tensor(rot[:, 1, :, 0:h2], heads[:, :, h2:ROT], per_head(ROT, ROT + h2), ALU.mult).then_inc(rope_part, 1)
                    pool.tensor_tensor(rot[:, 1, :, h2:ROT], heads[:, :, 0:h2], per_head(ROT + h2, 2 * ROT), ALU.mult).then_inc(rope_part, 1)
                    pool.wait_ge(rope_part, k + 3)
                    pool.tensor_tensor(heads[:, :, 0:ROT], rot[:, 0], rot[:, 1], ALU.add).then_inc(rope_done, 1)

            def convolve(i):
                k = (2 * CONV - 2) * i
                if i == 0:
                    pool.wait_ge(zero_done, 5)
                    pool.wait_ge(par_sb, 1)
                    pool.wait_ge(prep_v, 3)
                else:
                    pool.wait_ge(conv_done, i)
                for t in range(NT):
                    wait_event(pool, plan.ready["xr", 0, i // KT, t])
                if i >= 2:
                    pool.wait_ge(rg_dve, RG_DVE * (i - 1))
                tmp, x_i = prob[:, 1, :], rg_x[i % 2]

                def tap(j, dst):
                    col = C_CW + AT * j + i
                    args = (par[:, col:col + 1], par[:, C_CB + i:C_CB + i + 1], ALU.mult, ALU.add) if j == 0 else \
                        (par[:, col:col + 1], None, ALU.mult)
                    pool.tensor_scalar(dst, xrT[:, i, j:j + T], *args).then_inc(conv_part, 1)
                tap(0, x_i)
                for j in range(1, CONV):
                    tap(j, tmp)
                    pool.wait_ge(conv_part, k + 2 * j)
                    pool.tensor_tensor(x_i, x_i, tmp, ALU.add).then_inc(conv_done if j == CONV - 1 else conv_part, 1)
                    if j < CONV - 1:
                        pool.wait_ge(conv_part, k + 2 * j + 1)

            def both(i):
                pool.wait_ge(rg_dve, RG_DVE * i + 7)
                pool.tensor_tensor(rg_r[:, 0, :], rg_h[:, 0, :], rg_h[:, 1, :], ALU.add).then_inc(rg_sum, 1)

            def task_of(task):
                if task.kind == "upd":
                    gained(task)
                elif task.kind == "rsum":
                    rsqrt(2 * task.b, rstd_x, var_x)
                elif task.kind == "norm":
                    rsqrt(2 * task.b - 1, rstd_y, var_y)
                elif task.kind == "evac" and task.what in ("q", "k"):
                    rotate(task)
                elif task.kind == "rg0":
                    convolve(task.i)
                elif task.kind == "rg2":
                    both(task.i)
                elif task.kind == "heads":
                    pool.wait_ge(sub_var_done, task.g + 1)
                    pool.tensor_tensor(sub_r, sub_var, minus_half, ALU.pow).then_inc(sub_rstd, 1)
                if task.kind == "upd" and task.b == 0 and task.c == NC - 1 and task.t == NT - 1:
                    pool.wait_ge(xg_done, 8)
                    pool.memset(xrT[:, :, 0:CONV // 2], 0.0).then_inc(zero_done, 1)
                    pool.memset(xrT[:, :, CONV // 2 + T:XP], 0.0).then_inc(zero_done, 1)

            for part in plan.parts:
                if part.kind == "mixer":
                    for slot in part.slots:
                        for task in slot.pre + slot.post:
                            task_of(task)
                    continue
                for slot in part.head:
                    for task in slot.pre + slot.post:
                        task_of(task)
                rsqrt(2 * part.b + 1, rstd_y, var_y)


def log_counts():
    pairs = ((128, 1), (512, 4), (2048, 16))
    t, k = np.meshgrid(np.arange(T), np.arange(T), indexing="ij")
    count = sum(((t - k) % d == 0) & (abs(t - k) <= w // 2) for w, d in pairs)
    return np.where(count > 0, np.log(np.maximum(count, 1)) / SCALE, NEG).astype(np.float32)


def rope_tables():
    inv = np.float32(500000.0) ** (-np.arange(0, ROT, 2, dtype=np.float32) / np.float32(ROT))
    angle = (np.arange(T, dtype=np.float32)[:, None] * inv[None, :]).astype(np.float32)
    cos, sin = np.cos(angle), np.sin(angle)
    return np.concatenate([cos, cos, -sin, sin], axis=1).astype(np.float32)


_INS = ["x", "norm_mix_pre", "norm_mix_post", "norm_ffn_pre", "norm_ffn_post", "ev_w_in", "ev_conv_w", "ev_conv_b",
        "ev_w_r", "ev_b_r", "ev_w_i", "ev_b_i", "ev_lam", "ev_w_out", "od_w_in", "od_lam_q1", "od_lam_k1",
        "od_lam_q2", "od_lam_k2", "od_subln", "od_w_out", "ffn_w_gate", "ffn_w_up", "ffn_w_down"]


def kernel(**inputs):
    import concourse.bacc as bacc
    from concourse.bass_utils import run_bass_kernel_spmd

    nc = bacc.Bacc("TRN2", target_bir_lowering=False, num_devices=1, dynamic_dma_scratch_size=SCRATCH)
    arrays = {name: np.ascontiguousarray(inputs[name]) for name in _INS}
    arrays["log_count"] = log_counts()
    arrays["rope"] = rope_tables()
    arrays["identity"] = np.eye(P, dtype=np.float32)
    args = [nc.dram_tensor(f"in_{n}", a.shape, mybir.dt.from_np(a.dtype), kind="ExternalInput").ap()
            for n, a in arrays.items()]
    args.append(nc.dram_tensor("out_0", arrays["x"].shape, F32, kind="ExternalOutput").ap())
    trunk(nc, *args)
    result = run_bass_kernel_spmd(nc, [{f"in_{n}": a for n, a in arrays.items()}], core_ids=[0])
    return result.results[0]["out_0"]
```

```python
import math
from contextlib import ExitStack

import numpy as np

import concourse.bass as bass
from concourse import mybir

F32 = mybir.dt.float32
F32R = mybir.dt.float32r
BF16 = mybir.dt.bfloat16
ALU = mybir.AluOpType
ACT = mybir.ActivationFunctionType
AX = mybir.AxisListType

P = 128
T = 256
NT = T // P
D = 2048
KC = 512
KT = KC // P
NC = D // KC
EPS = 1e-6
NEG = -1e30
HD = 64
SCALE = HD ** -0.5
ROT = HD // 4
AW = D // 2
AT = AW // P
CONV = 4
DFF = -(-8 * D // (3 * 256)) * 256
NF = DFF // KC
CV = 2 * HD
LAM_INIT = 0.8 - 0.6 * math.exp(-0.3)
SCRATCH = 1024
RAW, HI, LO = 3, 4, 3
HI_LEAD, LO_LEAD = 3, 2
PAR_SLOT = 6
XP = T + CONV - 1
PAR = 3 * 2 * AT + (CONV + 1) * AT
C_LAM, C_BR, C_BI, C_CW, C_CB = 0, 2 * AT, 4 * AT, 6 * AT, 6 * AT + CONV * AT
HEADS_OF_GROUP = 8
SERIES = 9


class Task:

    def __init__(self, kind, b=0, layer=None, slot=None, k=(0, KT), src=None, what=None, g=0, t=0, c=0, i=0,
                 n=0, u=0, s=0, head=0, head_free=0, v_group=0, evac=None):
        self.kind, self.b, self.layer = kind, b, layer
        self.slot, self.k = slot, k
        self.src, self.what = src, what
        self.g, self.t, self.c, self.i = g, t, c, i
        self.n, self.u, self.s = n, u, s
        self.head, self.head_free, self.v_group, self.evac = head, head_free, v_group, evac
        self.rope = 0
        self.e = self.m = self.stat = self.sq = self.update = self.gained = None
        self.prev_pt = self.tok_free = self.stage_free = None


class Slot:

    def __init__(self, u, kg, n, first, last, w, cb=0, region="h", layer=0):
        self.u, self.n, self.first, self.last, self.layer = u, n, first, last, layer
        self.w, self.kg, self.cb, self.lhs = w, kg, cb, (region, kg)
        self.recurrent = w == "ev_out" and kg < 2
        self.adds, self.starts = w in ("ev_out", "od_out", "down"), w != "down" and kg == 0
        self.pre, self.early, self.mid, self.post = [], [], [], []
        self.b = self.block_e = None


class Body:

    def __init__(self, u, n, e, m, prev_gate):
        self.u, self.n, self.e, self.m, self.prev_up = u, n, e, m, prev_gate + 1


class Part:

    def __init__(self, layer=0, tasks=None, peeled=None, loop=None, tail=None):
        self.layer, self.tasks, self.peeled, self.loop, self.tail = layer, tasks, peeled, loop, tail


def ahead(u, lead):
    return u + 1 + min(lead, 1 + max(u, 0) // 2)


class Plan:

    def __init__(self):
        self.u = self.n = self.e = self.m = self.heads = self.ropes = 0
        self.stats = self.squares = self.updates = self.gains = self.y_gains = 0
        self.ready, self.read, self.pt, self.parts = {}, {}, {}, []
        self.stat, self.update, self.gained, self.y_gained = {}, {}, {}, {}

    def slot(self, w, kg, n, first, last, **where):
        self.u += 1
        return Slot(self.u - 1, kg, n, first, last, w, **where)


def mixer_slots(plan, layer):
    slots, evacs, b = [], {}, 2 * layer

    def unit(w, kg, cb, region, first, last):
        slots.append(plan.slot(w, kg, plan.n, first, last, cb=cb, region=region, layer=layer))
        plan.n += last

    if layer == 0:
        order = ([("xr", g, 2 + g) for g in range(2)] + [("gate", g, g) for g in range(2)]
                 + [(w, g, 4 + 2 * i + g) for g in range(2) for i, w in enumerate("qkv")])
        groups, w_in, w_out = 2, "ev_in", "ev_out"
    else:
        order = [(w, g, 4 * i + g) for g in range(4) for i, w in enumerate("qkv")]
        groups, w_in, w_out = 4, "od_in", "od_out"

    def put(slot, front=False, **what):
        task = Task(layer=layer, b=b, **what)
        slots[slot].post.insert(0, task) if front else slots[slot].post.append(task)
        return task

    for what, g, cb in order:
        for kg in range(NC):
            unit(w_in, kg, cb, "h", kg == 0, kg == NC - 1)
        s = len(slots) - 1
        head_free = plan.heads + HEADS_OF_GROUP * (g - 1) if g >= 2 else 0
        evacs[what, g] = put(s, kind="evac", what=what, g=g, n=slots[s].n, u=slots[s].u, s=s, head_free=head_free)
        if what in ("q", "k"):
            evacs[what, g].rope = plan.ropes
            plan.ropes += NT
    n_in = len(slots)
    for kg in range(NC):
        for cb in range(NC):
            unit(w_out, kg, cb, "y", True, True)

    for (what, g), evac in evacs.items():
        if what != "v":
            for t in range(NT):
                put(evac.s + 1 + (what in ("q", "k")), kind="T", src=what, g=g, t=t, evac=evac)
    starts = [evacs["v", g].s + 1 + 2 * (layer == 0 and g == 0) for g in range(groups)]
    for s in range(len(slots)):
        for kind, lag in (("s0", 0), ("pt", 1), ("pv", 2), ("s", 0)):
            for g, start in enumerate(starts):
                i = s - start - lag
                if 0 <= i < HEADS_OF_GROUP:
                    task = put(s, kind=kind, g=g, i=i, n=plan.heads + HEADS_OF_GROUP * g + i, v_group=evacs["v", g].n)
                    if kind == "pt" and layer == 1:
                        slots[s].early.append(Task("difference", n=task.n))
    for g, start in enumerate(starts):
        kg = g + 2 if layer == 0 else g
        last_head = plan.heads + HEADS_OF_GROUP * (g + 1) - 1
        if layer == 1:
            put(start + HEADS_OF_GROUP + 1, kind="heads", g=g)
            slots[start + HEADS_OF_GROUP + 2].early.append(Task("heads_scale", g=g))
        for t in range(NT):
            s = n_in if kg == 2 else start + HEADS_OF_GROUP + 2
            task = Task("T", b, layer, src="tok", g=kg, t=t, head=last_head)
            slots[s].post.insert(t if kg == 2 else len(slots[s].post), task)
    plan.heads += HEADS_OF_GROUP * groups
    if layer == 0:
        slot_of = [(12, 17, 21, 25)[i // 2] + i % 2 for i in range(AT)]
        for i, s in enumerate(slot_of):
            put(s - 2, kind="rg_conv", i=i)
            put(s, kind="rg_gates", i=i)
            if i % 2 == 0:
                for j in range(2):
                    put(s + 2, kind="rg_root", i=i + j)
            put(s + 2, kind="rg_scan", i=i)
            if i + 2 < AT:
                put(s + RAW + 1, kind="gate_weights", i=i + 2)
        for i, s in enumerate(slot_of):
            put(s + 3, front=True, kind="rg_out", i=i)
        for c in range(1, NC):
            slots[c - 1].mid.append(Task("input", c=c))
        put(PAR_SLOT, kind="load_parameters")
        for i in range(2):
            put(PAR_SLOT + 2, kind="gate_weights", i=i)
        for i in range(4):
            put(PAR_SLOT + i, kind="par", i=i)
    put(len(slots) - 12, kind="gains")
    slots[-12].post[-1].b = b + 1
    return slots


def half(slot, t, *between):
    if not between:
        return [Task("half", slot=slot, t=t)]
    return [Task("half", slot=slot, t=t, k=(0, 1)), *between, Task("half", slot=slot, t=t, k=(1, KT))]


def hi(u):
    return Task("hi", u=u)


def lo(u):
    return Task("lo", u=u)


def add_output(slot, t):
    return [Task("add_output", slot=slot, t=t)] if slot.adds else []


def run(slots):
    tasks = []
    for s in slots:
        tasks += s.pre + half(s, 0) + s.early
        tasks += [hi(u) for u in range(ahead(s.u - 1, HI_LEAD), ahead(s.u, HI_LEAD))]
        tasks += [lo(u) for u in range(ahead(s.u - 1, LO_LEAD), ahead(s.u, LO_LEAD))]
        tasks += add_output(s, 0) + s.mid + half(s, 1) + add_output(s, 1) + s.post
    return tasks


def boundary_tasks(b):
    return (lambda c, t: Task("update", b, c=c, t=t), lambda c, t: Task("T", b, src="x", g=c, t=t),
            lambda c, t: Task("square", b, c=c, t=t))


def first_boundary(slots):
    update, turn, square = boundary_tasks(0)
    for c in range(NC - 1):
        slots[c].mid += [turn(c + 1, t) for t in range(NT)]
        chunks = [0, 1] if c == 0 else [c + 1]
        post = [square(c2, t) for c2 in chunks for t in range(NT)]
        if c + 2 < NC:
            post = [update(c + 2, t) for t in range(NT)] + post
        else:
            post.append(Task("rms_x", 0))
        slots[c].post = post + slots[c].post
    start = [Task("first_half"), update(0, 0), turn(0, 0), hi(0), lo(0), update(0, 1), update(1, 0), update(1, 1)]
    start += half(slots[0], 0, turn(0, 1))
    return start + run(slots)[1:]


def boundary(b, before, after):
    update, turn, square = boundary_tasks(b)
    s0, s1, s2, s3 = before
    u = s0.u

    def y_square(slot, t):
        return Task("y_square", b, slot=slot, t=t)

    def rms_y(t):
        return Task("rms_y", b, t=t)

    def y_gain(c, t):
        return Task("y_gain", b, c=c, t=t)
    tasks = half(s0, 0) + [hi(u + 3), lo(u + 2)] + half(s1, 0) + add_output(s0, 0) + [y_square(s0, 0), y_gain(0, 0)]
    tasks += half(s2, 0) + add_output(s1, 0) + [y_square(s1, 0), y_gain(1, 0)] + half(s0, 1)
    tasks += ([hi(u + 4)] if after else []) + [lo(u + 3)] + add_output(s2, 0) + add_output(s0, 1)
    tasks += [y_square(s2, 0), y_gain(2, 0), y_square(s0, 1), y_gain(0, 1)] + half(s1, 1)
    tasks += [hi(u + 5), lo(u + 4)] if after else []
    tasks += add_output(s1, 1) + [y_square(s1, 1)] + half(s3, 0) + half(s2, 1)
    tasks += add_output(s3, 0) + [y_square(s3, 0), rms_y(0), update(0, 0)] + add_output(s2, 1)
    if not after:
        tasks += [y_gain(3, 0), update(1, 0), Task("store", c=0, t=0), y_square(s2, 1), update(2, 0), update(3, 0)]
        tasks += [Task("store", c=2, t=0), y_gain(1, 1), y_gain(2, 1)] + half(s3, 1) + add_output(s3, 1)
        tasks += [y_square(s3, 1), rms_y(1), y_gain(3, 1)]
        for c in (0, 2):
            tasks += [update(c, 1), update(c + 1, 1), Task("store", c=c, t=1)]
        return tasks
    e, f, g, h = after
    tasks += [hi(u + 6), update(1, 0), y_square(s2, 1)] + half(s3, 1) + add_output(s3, 1)
    tasks += [turn(0, 0), y_square(s3, 1), rms_y(1), y_gain(1, 1), lo(u + 5), update(0, 1)]
    tasks += half(e, 0, turn(1, 0)) + [hi(u + 7), update(1, 1)]
    tasks += half(f, 0, turn(0, 1)) + [y_gain(2, 1), square(0, 0), update(2, 0)]
    tasks += half(e, 1, turn(1, 1)) + [y_gain(3, 0), square(1, 0), square(0, 1), lo(u + 6), update(2, 1)]
    tasks += half(f, 1, turn(2, 0)) + [y_gain(3, 1), hi(u + 8), square(1, 1), update(3, 0), lo(u + 7)]
    tasks += half(g, 0, turn(2, 1)) + [hi(u + 9), update(3, 1), lo(u + 8)]
    tasks += half(g, 1, turn(3, 0)) + [square(2, 0), square(2, 1), square(3, 0)]
    tasks += half(h, 0, turn(3, 1)) + [square(3, 1), Task("rms_x", b), hi(u + 10), lo(u + 9)] + half(h, 1) + h.post
    return tasks


def number(plan, tasks):
    for task in tasks:
        if task.kind == "T":
            task.e = plan.e
            plan.e += 1
            buffer = "tok" if task.src == "tok" or (task.src == "x" and task.g % 2 == 0) else "stage"
            plan.read[buffer, task.t] = task.e
            key = {"x": ("x", task.b), "tok": ("y", task.layer)}.get(task.src, (task.src, task.layer))
            plan.ready[(*key, task.g, task.t)] = task.e
            if task.src in ("x", "tok"):
                task.m = plan.m
                plan.m += 1
            if task.src == "x":
                task.gained = plan.gained[task.b, task.g, task.t]
        elif task.kind == "pt":
            task.e = plan.e
            plan.e += 1
            plan.pt[task.n] = task.e
        elif task.kind in ("rms_x", "rms_y"):
            task.stat, task.sq = plan.stats, plan.squares
            plan.stat[task.kind, task.b, task.t] = plan.stats
            plan.stats += 1
        elif task.kind in ("square", "y_square"):
            task.sq, task.update = plan.squares, plan.update.get((task.b, task.c, task.t))
            task.stat = plan.stat.get(("rms_x", task.b - 1, 0))
            plan.squares += 1
        elif task.kind == "y_gain":
            task.sq, task.gained = plan.squares, plan.y_gains
            plan.y_gained[task.b, task.c, task.t] = plan.y_gains
            plan.y_gains += 1
        if task.kind in ("evac", "silu"):
            task.stat = plan.stat["rms_x", task.b, 0]
        if task.kind == "update":
            if task.b:
                task.stat, task.update = plan.stat["rms_y", task.b, task.t], plan.updates
                task.m = plan.y_gained[task.b, task.c, task.t]
                plan.update[task.b, task.c, task.t] = plan.updates
                plan.updates += 1
            task.gained = plan.gained[task.b, task.c, task.t] = plan.gains
            plan.gains += 1
        if task.kind in ("evac", "update", "pv", "s", "silu", "gate_up"):
            task.tok_free = [plan.read.get(("tok", t)) for t in range(NT)]
            task.stage_free = [plan.read.get(("stage", t)) for t in range(NT)]
        if task.kind == "s":
            task.prev_pt = plan.pt.get(task.n - 1)
        if task.kind == "half" and not task.slot.recurrent:
            region, kg = task.slot.lhs
            key = ("x", task.slot.b) if region == "h" else ("y", task.slot.layer)
            task.e = task.slot.block_e + task.t if task.slot.w == "down" else plan.ready[(*key, kg, task.t)]


def make_plan():
    plan, before = Plan(), None
    for layer in range(2):
        slots = mixer_slots(plan, layer)
        n_gate, n_up = plan.n, plan.n + 1
        head = [plan.slot(w, kg, n, kg == 0, kg == NC - 1, layer=layer)
                for w, n in (("gate", n_gate), ("up", n_up)) for kg in range(NC)]
        for b, part in ((2 * layer, slots), (2 * layer + 1, head)):
            for slot in part:
                slot.b = b
        head[NC - 1].post.append(Task("silu", 2 * layer + 1, n=n_gate, u=head[NC - 1].u))
        head[-1].post += [Task("gate_up", n=n_gate, u=head[-1].u), Task("gains", 2 * layer + 2)]
        start = boundary(2 * layer, before, slots[:NC]) if before else first_boundary(slots[:NC])
        tasks = (start + run(slots[NC:-NC]) + boundary(2 * layer + 1, slots[-NC:], head[:NC]) + run(head[NC:]))
        number(plan, tasks)
        plan.parts.append(Part(layer, tasks=tasks))
        u1, n1 = plan.u, plan.n + 2
        plan.parts.append(Part(
            layer, peeled=Body(u1, n1, plan.e, plan.m, n_gate),
            loop=Body(u1 + 12, n1 + 6, plan.e + NT, plan.m + NT, n1),
            tail=Body(u1 + 12 * (NF - 1), n1 + 6 * (NF - 1), plan.e + NT * (NF - 1), plan.m + NT * (NF - 1),
                      n1 + 6 * (NF - 2))))
        assert plan.e % 2 == 0 and plan.n % 2 == 0 and all(12 % ring == 0 for ring in (RAW, HI, LO))
        plan.u += 12 * (NF - 1)
        plan.n += 6 * NF
        plan.e += NT * NF
        plan.m += NT * NF
        for t in range(NT):
            plan.read["tok", t] = plan.e - NT + t
        before = [plan.slot("down", 0, plan.n - NC + cb, True, True, cb=cb, region="y", layer=layer) for cb in range(NC)]
        for slot in before:
            slot.block_e = plan.e - NT
    tasks = boundary(4, before, [])
    number(plan, tasks)
    plan.parts.append(Part(tasks=tasks))
    return plan


def trunk(nc, x, norm_mix_pre, norm_mix_post, norm_ffn_pre, norm_ffn_post,
          ev_w_in, ev_conv_w, ev_conv_b, ev_w_r, ev_b_r, ev_w_i, ev_b_i, ev_lam, ev_w_out,
          od_w_in, od_lam_q1, od_lam_k1, od_lam_q2, od_lam_k2, od_subln, od_w_out,
          ffn_w_gate, ffn_w_up, ffn_w_down, log_count, rope, identity, out):
    plan = make_plan()
    weights = {"ev_in": [ev_w_in[0]], "ev_out": [ev_w_out[0]], "od_in": [None, od_w_in[0]],
               "od_out": [None, od_w_out[0]], "gate": ffn_w_gate, "up": ffn_w_up, "down": ffn_w_down}
    x_rows = x[0].rearrange("(t p) d -> p t d", p=P)
    out_rows = out[0].rearrange("(t p) d -> p t d", p=P)

    with ExitStack() as ctx:
        def sb(name, shape, dt=F32):
            return ctx.enter_context(nc.sbuf_tensor(name, shape, dt))

        def sem(name):
            return ctx.enter_context(nc.semaphore(name))

        raw = [sb(f"raw{i}", [P, KT, KC]) for i in range(RAW)]
        w_hi = [sb(f"w_hi{i}", [P, KT, KC], F32R) for i in range(HI)]
        w_lo = [sb(f"w_lo{i}", [P, KT, KC], F32R) for i in range(LO)]
        xs = sb("xs", [P, NT, D])
        yacc = sb("yacc", [P, NT, D])
        h_hi = sb("h_hi", [P, D // P, T], F32R)
        h_lo = sb("h_lo", [P, D // P, T], F32R)
        y_hi = sb("y_hi", [P, 2 * KT, T], F32R)
        y_lo = sb("y_lo", [P, 2 * KT, T], F32R)
        tok = sb("tok", [P, NT, KC])
        stage = sb("stage", [P, NT, KC])
        gx = sb("gx", [P, max(AT * XP, D)])
        gq = sb("gq", [P, D])
        qT = [sb(f"qT{i}", [P, KT, T]) for i in range(2)]
        kT = [sb(f"kT{i}", [P, KT, T]) for i in range(2)]
        vb = [sb(f"vb{i}", [P, NT, KC]) for i in range(2)]
        prob = sb("prob", [P, 2, T])
        probT = sb("probT", [P, 2, T])
        packed = probT[:, 0, 0:P]
        logc = sb("logc", [P, NT, T])
        ropes = sb("ropes", [P, NT, 4 * (ROT // 2)])
        ident = sb("ident", [P, P])
        sub_gain = sb("sub_gain", [P, CV])
        junk = sb("junk", [P, KC], BF16)
        par = sb("par", [P, PAR])
        rot = sb("rot", [P, 2, KC // HD, ROT])
        lqk = rot[:, :, :, :].rearrange("p a b c -> p (a b c)")
        hc = sb("hc", [P, 2, 2 * AT])
        poly = sb("poly", [P, 4, 2 * AT])
        small = sb("small", [P, 72])

        pre_gain, post_gain = gx[:, 0:D], gq[:, :]
        xrT = gx[:, 0:AT * XP].rearrange("p (i t) -> p i t", i=AT)
        rg_w = [gq[:, 512 * i:512 * (i + 1)].rearrange("p (g f) -> p g f", g=4) for i in range(2)]
        rg_x = [gq[:, 1024 + T * i:1024 + T * (i + 1)] for i in range(2)]
        rg_h = gq[:, 1536:2048].rearrange("p (d t) -> p d t", d=2)
        flat = yacc[:, :, :].rearrange("p t d -> p (t d)")
        halves = [flat[:, 2048 + 512 * i:2560 + 512 * i] for i in range(4)]
        for buf in (qT[1], kT[1]):
            flat_buf = buf[:, :, :].rearrange("p k t -> p (k t)")
            halves += [flat_buf[:, 0:512], flat_buf[:, 512:1024]]
        halves = [part.rearrange("p (d t) -> p d t", d=2) for part in halves]
        rg_r, rg_i, rg_a, rg_t = [[halves[i], halves[4 + i]] for i in range(4)]
        geluT = flat[:, 0:AT * T].rearrange("p (i t) -> p i t", i=AT)
        ss_y, ss_x = small[:, 0:8].rearrange("p (t c) -> p t c", t=2), small[:, 8:16].rearrange("p (t c) -> p t c", t=2)
        var_y, var_x, rstd_y, rstd_x = small[:, 16:18], small[:, 18:20], small[:, 20:22], small[:, 22:24]
        mx, nmx = small[:, 24:26], small[:, 26:28]
        den = [small[:, 28 + 2 * i:30 + 2 * i] for i in range(2)]
        rden = small[:, 32:34]
        nlam, lam_e, lam_s = small[:, 34:35], small[:, 36:38], small[:, 38:40]
        sub_ss, sub_var, sub_r = small[:, 40:48], small[:, 48:56], small[:, 56:64]
        minus_half = small[:, 64:72]

        acc = [[ctx.enter_context(nc.psum_tensor(f"acc{i}{t}", [P, KC], F32)) for t in range(NT)] for i in range(2)]
        tp = [ctx.enter_context(nc.psum_tensor(f"tp{i}", [P, KT, P], F32)) for i in range(2)]
        sc = ctx.enter_context(nc.psum_tensor("sc", [P, 2, T], F32))
        pv = ctx.enter_context(nc.psum_tensor("pv", [P, 2, T], F32))

        landed = [sem(f"landed{i}") for i in range(RAW)]
        first_landed = sem("first_landed")
        first_hi = sem("first_hi")
        first_lo = sem("first_lo")
        hi_done = sem("hi_done")
        lo_done = sem("lo_done")
        half_done = sem("half_done")
        unit_done = sem("unit_done")
        acc_free = [[sem(f"acc_free{i}{t}") for t in range(NT)] for i in range(2)]
        tp_done = sem("tp_done")
        tp_free = [sem(f"tp_free{i}") for i in range(2)]
        t_hi = sem("t_hi")
        ident_in = sem("ident_in")
        x_in = [sem(f"x_in{c}") for c in range(NC)]
        par_in = sem("par_in")
        gain_in = [sem(f"gain_in{i}") for i in range(2)]
        rgw_in = [sem(f"rgw_in{i}") for i in range(2)]
        stored = sem("stored")
        sq_done = sem("sq_done")
        var_done = sem("var_done")
        var_part = sem("var_part")
        rstd_done = sem("rstd_done")
        yg_done = sem("yg_done")
        upd_done = sem("upd_done")
        xg_done = sem("xg_done")
        rope_part = sem("rope_part")
        rope_done = sem("rope_done")
        s0_done = sem("s0_done")
        s_done = sem("s_done")
        max_part = sem("max_part")
        nmx_done = sem("nmx_done")
        s_free = sem("s_free")
        exp_done = sem("exp_done")
        att_part = sem("att_part")
        att_done = sem("att_done")
        pv_done = sem("pv_done")
        sub_sq = sem("sub_sq")
        sub_var_done = sem("sub_var_done")
        sub_rstd = sem("sub_rstd")
        heads_done = sem("heads_done")
        rden_done = sem("rden_done")
        o_done = sem("o_done")
        zero_done = sem("zero_done")
        par_T = sem("par_T")
        par_sb = sem("par_sb")
        prep_a = sem("prep_a")
        prep_v = sem("prep_v")
        conv_part = sem("conv_part")
        conv_done = sem("conv_done")
        gates_done = sem("gates_done")
        rg_act = sem("rg_act")
        rg_decay = sem("rg_decay")
        rg_root_done = sem("rg_root_done")
        rg_scan = sem("rg_scan")
        rg_out = sem("rg_out")
        rg_sum = sem("rg_sum")
        rg_hi = sem("rg_hi")

        RG_ACT, RG_DECAY, RG_SCAN, RG_OUT = 8, 2, 5, 2
        PREP = 25
        block = ctx.enter_context(nc.Block())

        def wait_event(eng, e):
            eng.wait_ge(tp_free[e % 2], e // 2 + 1)

        def wait_acc(eng, n, t):
            eng.wait_ge(acc_free[n % 2][t], n // 2 + 1)

        def wait_product(eng, u, t, off=0):
            eng.wait_ge(unit_done if t else half_done, u + 1 + off)

        def operand(lhs, hi, k, t):
            region, kg = lhs
            if region == "y" and kg < 2:
                src = y_hi if hi else y_lo
            else:
                src, kg = (h_hi if hi else h_lo), kg - 2 * (region == "y")
            return src[:, kg * KT + k, t * P:(t + 1) * P]

        def region_of(task):
            t = task.t
            if task.src == "x" or task.g >= 2:
                kt = KT * (task.g if task.src == "x" else task.g - 2)
                return [b[:, kt:kt + KT, t * P:(t + 1) * P] for b in (h_hi, h_lo)]
            return [b[:, KT * task.g:KT * (task.g + 1), t * P:(t + 1) * P] for b in (y_hi, y_lo)]

        def x_buffer(c):
            return tok if c % 2 == 0 else stage

        @block.sync
        def _(sp):
            def load_first(src):
                for ks, landed_half in ((slice(0, KT // 2), first_landed), (slice(KT // 2, KT), landed[0])):
                    sp.dma_start(raw[0][:, ks, :], src.rearrange("(k p) n -> p k n", p=P)[:, ks, :]).then_inc(landed_half, 16)

            def load(u, src, it=0):
                if u >= RAW:
                    sp.wait_ge(lo_done, u - RAW + 1 + 12 * it)
                sp.dma_start(raw[u % RAW][:, :, :], src.rearrange("(k p) n -> p k n", p=P)).then_inc(landed[u % RAW], 16)

            def input_chunk(c):
                cols = slice(c * KC, (c + 1) * KC)
                sp.dma_start(xs[:, :, cols], x_rows[:, :, cols]).then_inc(x_in[c], 16)
                sp.dma_start(pre_gain[:, cols], norm_mix_pre[0, cols].partition_broadcast(P)).then_inc(x_in[c], 16)

            def load_parameters():
                for row, src in ((C_LAM, ev_lam[0].rearrange("d (i p) -> (d i) p", p=P)),
                                 (C_BR, ev_b_r[0].rearrange("d (i p) -> (d i) p", p=P)),
                                 (C_BI, ev_b_i[0].rearrange("d (i p) -> (d i) p", p=P)),
                                 (C_CW, ev_conv_w[0].rearrange("j (i p) -> (j i) p", p=P)),
                                 (C_CB, ev_conv_b[0].rearrange("(i p) -> i p", p=P))):
                    sp.dma_start(packed[row:row + src.shape[0], :], src).then_inc(par_in, 16)
                for i, src in enumerate((od_lam_q1, od_lam_k1, od_lam_q2, od_lam_k2)):
                    sp.dma_start(lqk[:, HD * i:HD * (i + 1)], src[0].partition_broadcast(P)).then_inc(par_in, 16)
                sp.dma_start(sub_gain[:, :], od_subln[0].partition_broadcast(P)).then_inc(par_in, 16)
                sp.dma_start(logc[:, :, :], log_count.rearrange("(t p) k -> p t k", p=P)).then_inc(par_in, 16)
                sp.dma_start(ropes[:, :, :], rope.rearrange("(t p) k -> p t k", p=P)).then_inc(par_in, 16)

            def recurrence_weights(i):
                for j, w in enumerate((ev_w_r, ev_w_i)):
                    for half in range(2):
                        p0 = HD * half
                        sp.dma_start(rg_w[i % 2][p0:p0 + HD, 2 * j:2 * j + 2, p0:p0 + HD],
                                      w[0, :, 2 * i + half].rearrange("d e f -> e d f")).then_inc(rgw_in[i % 2], 16)

            def gains(b):
                if b == 1:
                    sp.wait_ge(rg_out, RG_OUT * AT)
                else:
                    sp.wait_ge(yg_done, 8 * (b - 1))
                    sp.wait_ge(xg_done, 8 * b)
                post = norm_mix_post[b // 2] if b % 2 else norm_ffn_post[b // 2 - 1]
                sp.dma_start(post_gain, post.partition_broadcast(P)).then_inc(gain_in[0], 16)
                if b < 4:
                    pre = norm_ffn_pre[b // 2] if b % 2 else norm_mix_pre[b // 2]
                    sp.dma_start(pre_gain, pre.partition_broadcast(P)).then_inc(gain_in[1], 16)

            def load_slot(slot):
                block = NF - 1 if slot.w == "down" else slot.kg
                rows = slice(block * KC, (block + 1) * KC)
                src = weights[slot.w][slot.layer][rows, slot.cb * KC:(slot.cb + 1) * KC]
                if slot.u:
                    load(slot.u, src)
                else:
                    input_chunk(0)
                    sp.dma_start(ident[:, :], identity).then_inc(ident_in, 16)
                    load_first(src)

            def task_of(task):
                if task.kind == "half" and task.t == 0 and task.k[0] == 0:
                    load_slot(task.slot)
                elif task.kind == "gains":
                    gains(task.b)
                elif task.kind == "input":
                    input_chunk(task.c)
                elif task.kind == "load_parameters":
                    load_parameters()
                elif task.kind == "gate_weights":
                    if task.i < 2:
                        sp.wait_ge(zero_done, 3)
                    else:
                        sp.wait_ge(gates_done, task.i - 1)
                    recurrence_weights(task.i)
                elif task.kind == "store":
                    cols = slice(task.c * KC, (task.c + 2) * KC)
                    sp.wait_ge(upd_done, plan.update[4, task.c + 1, task.t] + 1)
                    sp.dma_start(out_rows[:, task.t, cols], xs[:, task.t, cols]).then_inc(stored, 16)

            for part in plan.parts:
                if part.tasks:
                    for task in part.tasks:
                        task_of(task)
                    continue
                wg, wu, wd = (weights[w][part.layer] for w in ("gate", "up", "down"))

                def body(base, cols, rows, it=0):
                    for i in range(2 * NC):
                        load(base.u + i, (wg if i < NC else wu)[(i % NC) * KC:(i % NC + 1) * KC, cols], it)
                    for cb in range(NC):
                        load(base.u + 2 * NC + cb, wd[rows, cb * KC:(cb + 1) * KC], it)

                body(part.peeled, slice(KC, 2 * KC), slice(0, KC))
                with sp.Fori(0, NF - 2) as it:
                    body(part.loop, bass.ds(it * KC + 2 * KC, KC), bass.ds(it * KC + KC, KC), it)
            sp.wait_ge(stored, 16 * NC)

        @block.scalar
        def _(act):
            def first_half():
                act.wait_ge(first_landed, 16)
                act.activation(w_hi[0][:, 0:KT // 2, :], raw[0][:, 0:KT // 2, :], ACT.Copy).then_inc(first_hi, 1)

            def rest_of_first():
                act.wait_ge(landed[0], 16)
                act.activation(w_hi[0][:, KT // 2:KT, :], raw[0][:, KT // 2:KT, :], ACT.Copy).then_inc(hi_done, 1)

            def hi(u, it=0):
                act.wait_ge(landed[u % RAW], 16 * (u // RAW + 1) + 16 * (12 // RAW) * it)
                if u >= HI:
                    act.wait_ge(unit_done, u - HI + 1 + 12 * it)
                act.activation(w_hi[u % HI][:, :, :], raw[u % RAW][:, :, :], ACT.Copy).then_inc(hi_done, 1)

            def square(task):
                if task.sq:
                    act.wait_ge(sq_done, task.sq)
                if task.kind == "y_square":
                    wait_acc(act, task.slot.n, task.t)
                    c, src, sums = task.slot.cb, yacc, ss_y
                elif task.b == 0:
                    act.wait_ge(x_in[task.c], 32)
                    c, src, sums = task.c, xs, ss_x
                else:
                    act.wait_ge(upd_done, task.update + 1)
                    act.wait_ge(var_done, task.stat + 1)
                    c, src, sums = task.c, xs, ss_x
                act.activation(junk[:, :], src[:, task.t, c * KC:(c + 1) * KC], ACT.Square,
                               accum_out=sums[:, task.t, c:c + 1]).then_inc(sq_done, 1)

            def operand_hi(task):
                act.wait_ge(tp_done, task.e + 1)
                act.activation(region_of(task)[0], tp[task.e % 2][:, :, :], ACT.Copy).then_inc(t_hi, 1)

            def evac(task):
                slot, n = task.n % 2, task.n
                for t in range(NT):
                    wait_product(act, task.u, t)
                    if t == 0:
                        act.wait_ge(rstd_done, task.stat + 1)
                    if task.what == "v":
                        if task.head_free:
                            act.wait_ge(o_done, task.head_free)
                        dst = vb[task.g % 2][:, t, :]
                    else:
                        if task.stage_free[t] is not None:
                            act.wait_ge(tp_done, task.stage_free[t] + 1)
                        dst = stage[:, t, :]
                    func = ACT.Gelu_apprx_tanh if task.what == "gate" else ACT.Copy
                    act.activation(dst, acc[slot][t][:, :], func, scale=rstd_x[:, t:t + 1]).then_inc(acc_free[slot][t], 1)

            def transposed(task):
                if task.src in ("x", "tok"):
                    operand_hi(task)
                    return
                act.wait_ge(tp_done, task.e + 1)
                t0 = task.t * P
                if task.src == "gate":
                    dst = geluT[:, KT * task.g:KT * (task.g + 1), t0:t0 + P]
                elif task.src == "xr":
                    if task.g == 0 and task.t == 0:
                        act.wait_ge(xg_done, 8)
                    dst = xrT[:, KT * task.g:KT * (task.g + 1), CONV // 2 + t0:CONV // 2 + t0 + P]
                else:
                    if task.evac.head_free:
                        act.wait_ge(o_done, task.evac.head_free)
                    if task.layer == 0 and task.g == 1:
                        act.wait_ge(rg_out, RG_OUT * AT)
                    dst = (qT if task.src == "q" else kT)[task.g % 2][:, :, t0:t0 + P]
                act.activation(dst, tp[task.e % 2][:, :, :], ACT.Copy).then_inc(tp_free[task.e % 2], 1)

            def softmax(task):
                n = task.n
                act.wait_ge(nmx_done, n + 1)
                if n >= 2:
                    act.wait_ge(o_done, n - 1)
                if task.layer == 0:
                    for t in range(NT):
                        ins = act.activation(prob[:, t, :], prob[:, t, :], ACT.Exp, scale=SCALE, bias=nmx[:, t:t + 1],
                                             accum_out=den[n % 2][:, t:t + 1])
                    ins.then_inc(exp_done, 1)
                else:
                    act.wait_ge(tp_done, task.prev_pt + 1)
                    for m in range(2):
                        ins = act.activation(prob[:, m, :], sc[:, m, :], ACT.Exp, scale=SCALE, bias=nmx[:, m:m + 1],
                                             accum_out=den[n % 2][:, m:m + 1])
                    ins.then_inc(exp_done, 1)

            def prob_transposed(task):
                n = task.n
                act.wait_ge(tp_done, task.e + 1)
                if n:
                    act.wait_ge(pv_done, n)
                flat_tp = tp[task.e % 2][:, :, :].rearrange("p a b -> p (a b)")
                flat_pt = probT[:, :, :].rearrange("p a b -> p (a b)")
                cols = 2 * T if task.layer == 0 else T
                act.activation(flat_pt[:, 0:cols], flat_tp[:, 0:cols], ACT.Copy).then_inc(tp_free[task.e % 2], 1)

            def values(task):
                if task.layer == 1:
                    hd, t = task.i // 2, task.i % 2
                    act.wait_ge(o_done, task.n + 1)
                    if task.n > 16:
                        act.wait_ge(sub_sq, task.n - 16)
                    if task.i == 0 and task.g:
                        act.wait_ge(sub_var_done, task.g)
                    act.activation(probT[:, 1, 0:CV], tok[:, t, hd * CV:(hd + 1) * CV], ACT.Square,
                                   accum_out=sub_ss[:, task.i:task.i + 1]).then_inc(sub_sq, 1)

            def parameters(i):
                if i == 0:
                    act.wait_ge(par_T, 1)
                    act.activation(par[:, :], sc[:, :, :].rearrange("p a b -> p (a b)")[:, 0:PAR], ACT.Copy).then_inc(par_sb, 1)
                elif i == 1:
                    act.wait_ge(prep_v, 1)
                    act.activation(poly[:, 0, :], poly[:, 1, :], ACT.Exp, scale=-1.0).then_inc(prep_a, 1)
                    act.wait_ge(prep_v, 4)
                    act.activation(lam_e, lam_s, ACT.Exp).then_inc(prep_a, 1)

            def gates(i):
                act.wait_ge(gates_done, i + 1)
                if i == 0:
                    act.wait_ge(prep_v, PREP)
                if i >= 2:
                    act.wait_ge(rg_out, RG_OUT * (i - 1))
                r, gate_i, a, tanh = [buf[i % 2] for buf in (rg_r, rg_i, rg_a, rg_t)]
                for d in range(2):
                    col = AT * d + i
                    act.activation(r[:, d, :], sc[:, d, :], ACT.Tanh, scale=0.5, bias=par[:, C_BR + col:C_BR + col + 1]).then_inc(rg_act, 1)
                    act.activation(gate_i[:, d, :], pv[:, d, :], ACT.Tanh, scale=0.5, bias=par[:, C_BI + col:C_BI + col + 1]).then_inc(rg_act, 1)
                act.wait_ge(rg_act, RG_ACT * i + 4)
                for d in range(2):
                    col = AT * d + i
                    act.activation(a[:, d, :], r[:, d, :], ACT.Exp, scale=hc[:, 1, col:col + 1], bias=hc[:, 1, col:col + 1]).then_inc(rg_act, 1)
                    act.activation(tanh[:, d, :], r[:, d, :], ACT.Tanh, scale=hc[:, 0, col:col + 1], bias=hc[:, 0, col:col + 1]).then_inc(rg_act, 1)

            def root(i):
                act.wait_ge(rg_decay, RG_DECAY * (i + 1))
                t = rg_t[i % 2]
                act.activation(t[:, :, :], t[:, :, :], ACT.Sqrt).then_inc(rg_root_done, 1)

            def recurrence_hi(i):
                act.wait_ge(rg_out, RG_OUT * i + 1)
                act.activation(y_hi[:, i, :], rg_r[i % 2][:, 1, :], ACT.Copy).then_inc(rg_hi, 1)

            def task_of(task):
                if task.kind == "T":
                    transposed(task)
                elif task.kind in ("square", "y_square"):
                    square(task)
                elif task.kind == "hi":
                    hi(task.u) if task.u else rest_of_first()
                elif task.kind == "first_half":
                    first_half()
                elif task.kind == "silu":
                    act.wait_ge(rstd_done, task.stat + 1)
                    silu(task.n, task.u, lambda t: act.wait_ge(tp_done, task.stage_free[t] + 1))
                elif task.kind == "par":
                    parameters(task.i)
                elif task.kind == "evac":
                    evac(task)
                elif task.kind == "s":
                    softmax(task)
                elif task.kind == "pt":
                    prob_transposed(task)
                elif task.kind == "pv":
                    values(task)
                elif task.kind == "rg_gates":
                    gates(task.i)
                elif task.kind == "rg_root":
                    root(task.i)
                elif task.kind == "rg_out":
                    recurrence_hi(task.i)

            def silu(n, u, free, it=0):
                for t in range(NT):
                    wait_product(act, u, t, 12 * it)
                    free(t)
                    act.activation(stage[:, t, :], acc[n % 2][t][:, :], ACT.Silu, scale=rstd_x[:, t:t + 1]).then_inc(acc_free[n % 2][t], 1)

            def block_hi(base, it=0):
                for t in range(NT):
                    act.wait_ge(tp_done, base.e + t + 1 + NT * it)
                    act.activation(y_hi[:, 0:KT, t * P:(t + 1) * P], tp[t][:, :, :], ACT.Copy).then_inc(t_hi, 1)

            def body(base, it=0):
                block_hi(base, it)
                for i in range(12):
                    hi(base.u + i + HI_LEAD, it)
                    if i == NC - 1:
                        silu(base.n, base.u + i, lambda t: act.wait_ge(acc_free[base.prev_up % 2][t], base.prev_up // 2 + 1 + 3 * it), it)

            for part in plan.parts:
                if part.tasks:
                    for task in part.tasks:
                        task_of(task)
                    continue
                body(part.peeled)
                with act.Fori(0, NF - 2) as it:
                    body(part.loop, it)
                block_hi(part.tail)

        @block.tensor
        def _(pe):
            def product(u, n, lhs, first, last, t, k_tiles=(0, KT), it=0):
                hi_tile, lo_tile = w_hi[u % HI], w_lo[u % LO]
                if k_tiles[0] == 0:
                    if u:
                        pe.wait_ge(lo_done, u + 1 + 12 * it)
                    else:
                        pe.wait_ge(first_lo, 1)
                    if first and n >= 2:
                        pe.wait_ge(acc_free[n % 2][t], n // 2 + 3 * it)
                for k in range(*k_tiles):
                    if u == 0 and k == KT // 2:
                        pe.wait_ge(lo_done, 1)
                    for j, (a, w) in enumerate(((1, hi_tile), (1, lo_tile), (0, hi_tile))):
                        mm = pe.matmul(acc[n % 2][t][:, :], operand(lhs, a, k, t), w[:, k, :],
                                       start=first and k == 0 and j == 0, stop=last and k == KT - 1 and j == 2)
                if k_tiles[1] == KT:
                    mm.then_inc(unit_done if t else half_done, 1)

            def unit(u, n, lhs, first, last, it=0):
                for t in range(NT):
                    product(u, n, lhs, first, last, t, it=it)

            def transposes(e, pieces, off=0):
                if e >= 2:
                    pe.wait_ge(tp_free[e % 2], e // 2 + off)
                for dst, src in pieces:
                    ins = pe.transpose(dst, src, ident[:, :])
                ins.then_inc(tp_done, 1)

            def quarter(e, src, t):
                return [(tp[e % 2][:, k, :], src[:, t, k * P:(k + 1) * P]) for k in range(KT)]

            def task_of(task):
                if task.kind == "half":
                    slot = task.slot
                    if slot.recurrent:
                        pe.wait_ge(rg_out, RG_OUT * KT * (slot.kg + 1))
                    elif task.e is not None:
                        wait_event(pe, task.e)
                    product(slot.u, slot.n, slot.lhs, slot.first, slot.last, task.t, task.k)
                elif task.kind == "T":
                    if task.src == "x":
                        pe.wait_ge(xg_done, task.gained + 1)
                        src = x_buffer(task.g)
                    elif task.src == "tok":
                        if task.layer == 0:
                            pe.wait_ge(o_done, task.head + 1)
                        else:
                            pe.wait_ge(heads_done, task.g + 1)
                        src = tok
                    else:
                        src = stage
                        if task.src in ("q", "k"):
                            pe.wait_ge(rope_done, task.evac.rope + task.t + 1)
                        else:
                            wait_acc(pe, task.evac.n, task.t)
                    transposes(task.e, quarter(task.e, src, task.t))
                elif task.kind == "par" and task.i == 0:
                    pe.wait_ge(par_in, 16 * 12)
                    pe.transpose(sc[:, :, :].rearrange("p a b -> p (a b)")[:, 0:PAR], packed[0:PAR, :], ident[0:PAR, 0:PAR]).then_inc(par_T, 1)
                elif task.kind == "rg_gates":
                    i = task.i
                    pe.wait_ge(conv_done, i + 1)
                    pe.wait_ge(rgw_in[i % 2], 64 * (i // 2 + 1))
                    if i == 0:
                        pe.wait_ge(par_sb, 1)
                    else:
                        pe.wait_ge(rg_act, RG_ACT * (i - 1) + 4)
                    for j, bank in enumerate((sc, pv)):
                        for d in range(2):
                            mm = pe.matmul(bank[:, d, :], rg_w[i % 2][:, 2 * j + d, :], rg_x[i % 2], start=True, stop=True)
                    mm.then_inc(gates_done, 1)
                elif task.kind in ("s0", "s"):
                    n, j = task.n, int(task.kind == "s")
                    if j:
                        pe.wait_ge(s0_done, n + 1)
                    elif n > 16:
                        pe.wait_ge(exp_done, n)
                    elif n:
                        pe.wait_ge(s_free, n)
                    else:
                        pe.wait_ge(rg_act, RG_ACT * (AT - 1) + 4)
                    if task.i == 0:
                        for src in "qk":
                            for t in range(NT):
                                wait_event(pe, plan.ready[src, task.layer, task.g, t])
                    q, k = qT[task.g % 2], kT[task.g % 2]
                    if task.layer == 0:
                        r, kt, t = HD * (task.i % 2), task.i // 2, j
                    else:
                        r, kt, t = HD * j, task.i // 2, task.i % 2
                    pe.matmul(sc[:, j, :], q[r:r + HD, kt, t * P:(t + 1) * P], k[r:r + HD, kt, :],
                              start=True, stop=True).then_inc(s_done if j else s0_done, 1)
                elif task.kind == "pt":
                    if task.layer == 0:
                        pe.wait_ge(exp_done, task.n + 1)
                        flat_tp = tp[task.e % 2][:, :, :].rearrange("p a b -> p (a b)")
                        transposes(task.e, [(flat_tp[:, j * T + t * P:j * T + (t + 1) * P], prob[:, t, j * P:(j + 1) * P])
                                            for j in range(2) for t in range(NT)])
                    else:
                        pe.wait_ge(att_done, task.n - 16 + 1)
                        transposes(task.e, [(tp[task.e % 2][:, j, :], prob[:, 0, j * P:(j + 1) * P]) for j in range(2)])
                elif task.kind == "pv":
                    n = task.n
                    wait_event(pe, plan.pt[n])
                    if n:
                        pe.wait_ge(o_done, n)
                    if task.i == 0:
                        for t in range(NT):
                            wait_acc(pe, task.v_group, t)
                    v = vb[task.g % 2]
                    if task.layer == 0:
                        for t in range(NT):
                            for j in range(2):
                                mm = pe.matmul(pv[:, 0, t * HD:(t + 1) * HD], probT[:, j, t * P:(t + 1) * P],
                                               v[:, j, task.i * HD:(task.i + 1) * HD], start=j == 0, stop=j == 1)
                    else:
                        flat_pt, hd = probT[:, 0, :], task.i // 2
                        for j in range(2):
                            mm = pe.matmul(pv[:, 0, 0:CV], flat_pt[:, j * P:(j + 1) * P], v[:, j, hd * CV:(hd + 1) * CV],
                                           start=j == 0, stop=j == 1)
                    mm.then_inc(pv_done, 1)

            pe.wait_ge(ident_in, 16)
            for part in plan.parts:
                if part.tasks:
                    for task in part.tasks:
                        task_of(task)
                    continue

                def down_operand(base, it=0):
                    for t in range(NT):
                        pe.wait_ge(acc_free[base.prev_up % 2][t], base.prev_up // 2 + 1 + 3 * it)
                        transposes(base.e + t, quarter(base.e + t, tok, t), off=it)

                def down(u, n, base, it=0):
                    for t in range(NT):
                        pe.wait_ge(tp_free[t], base.e // 2 + 1 + it)
                    for cb in range(NC):
                        unit(u + cb, n + cb, ("y", 0), True, True, it)

                def body(base, it=0):
                    down_operand(base, it)
                    for i in range(2 * NC):
                        unit(base.u + i, base.n + i // NC, ("h", i % NC), i % NC == 0, i % NC == NC - 1, it)
                    down(base.u + 2 * NC, base.n + 2, base, it)

                body(part.peeled)
                with pe.Fori(0, NF - 2) as it:
                    body(part.loop, it)
                down_operand(part.tail)

        @block.vector
        def _(dve):
            def lo_first(ks):
                dve.tensor_tensor(w_lo[0][:, ks, :], raw[0][:, ks, :], w_hi[0][:, ks, :].bitcast(F32),
                                  ALU.subtract).then_inc(lo_done if ks.start else first_lo, 1)

            def lo(u, it=0):
                dve.wait_ge(hi_done, u + 1 + 12 * it)
                if u >= LO:
                    dve.wait_ge(unit_done, u - LO + 1 + 12 * it)
                dve.tensor_tensor(w_lo[u % LO][:, :, :], raw[u % RAW][:, :, :],
                                  w_hi[u % HI][:, :, :].bitcast(F32), ALU.subtract).then_inc(lo_done, 1)

            def operand_lo(e, m, hi_ap, lo_ap, it=0):
                dve.wait_ge(t_hi, m + 1 + NT * it)
                dve.tensor_tensor(lo_ap, tp[e % 2][:, :, :], hi_ap.bitcast(F32), ALU.subtract).then_inc(tp_free[e % 2], 1)

            def mean(task):
                if task.kind == "rms_x":
                    sums, var = ss_x, var_x
                else:
                    sums, var = ss_y[:, task.t, :], var_y[:, task.t:task.t + 1]
                dve.wait_ge(sq_done, task.sq)
                if task.stat >= 3:
                    dve.wait_ge(rstd_done, task.stat - 2)
                dve.tensor_reduce(var, sums, AX.X, ALU.add).then_inc(var_part, 1)
                dve.wait_ge(var_part, task.stat + 1)
                dve.tensor_scalar(var, var, 1.0 / D, EPS, ALU.mult, ALU.add).then_inc(var_done, 1)

            def update(task):
                if task.b == 0:
                    return
                if task.c == 0:
                    dve.wait_ge(rstd_done, task.stat + 1)
                dve.wait_ge(yg_done, task.m + 1)
                cols = slice(task.c * KC, (task.c + 1) * KC)
                r = xs[:, task.t, cols]
                dve.scalar_tensor_tensor(r, yacc[:, task.t, cols], rstd_y[:, task.t:task.t + 1], r,
                                         ALU.mult, ALU.add).then_inc(upd_done, 1)

            def add_output(n, u, cb, start, t, it=0):
                wait_product(dve, u, t, 12 * it)
                y, a = yacc[:, t, cb * KC:(cb + 1) * KC], acc[n % 2][t][:, :]
                if start:
                    dve.tensor_copy(y, a).then_inc(acc_free[n % 2][t], 1)
                else:
                    dve.tensor_tensor(y, a, y, ALU.add).then_inc(acc_free[n % 2][t], 1)

            def softmax(task):
                n = task.n
                dve.wait_ge(s_done, n + 1)
                if n:
                    dve.wait_ge(exp_done, n)
                if task.layer == 0:
                    if n:
                        dve.wait_ge(tp_done, task.prev_pt + 1)
                    for t in range(NT):
                        ins = dve.tensor_tensor_reduce(prob[:, t, :], sc[:, t, :], logc[:, t, :], 1.0, 3.0 * NEG,
                                                       ALU.add, ALU.max, mx[:, t:t + 1])
                    ins.then_inc(s_free, 1)
                    dve.wait_ge(s_free, n + 1)
                else:
                    dve.tensor_reduce(mx, sc[:, :, :], AX.X, ALU.max).then_inc(max_part, 1)
                    dve.wait_ge(max_part, n - 16 + 1)
                dve.tensor_scalar(nmx, mx, -SCALE, None, ALU.mult).then_inc(nmx_done, 1)

            def difference(task):
                n, k = task.n, 3 * (task.n - 16)
                dve.wait_ge(exp_done, n + 1)
                if k:
                    dve.wait_ge(att_done, n - 16)
                dve.reciprocal(rden, den[n % 2]).then_inc(att_part, 1)
                dve.wait_ge(att_part, k + 1)
                dve.tensor_tensor(rden[:, 1:2], rden[:, 1:2], nlam, ALU.mult).then_inc(att_part, 1)
                dve.tensor_scalar(prob[:, 0, :], prob[:, 0, :], rden[:, 0:1], None, ALU.mult).then_inc(att_part, 1)
                dve.wait_ge(att_part, k + 3)
                dve.scalar_tensor_tensor(prob[:, 0, :], prob[:, 1, :], rden[:, 1:2], prob[:, 0, :], ALU.mult, ALU.add).then_inc(att_done, 1)

            def values(task):
                n = task.n
                dve.wait_ge(pv_done, n + 1)
                for t in range(NT):
                    if task.i == 0 and task.tok_free[t] is not None:
                        dve.wait_ge(tp_done, task.tok_free[t] + 1)
                if task.layer == 0:
                    if n:
                        dve.wait_ge(o_done, n)
                    dve.reciprocal(rden, den[n % 2]).then_inc(rden_done, 1)
                    dve.wait_ge(rden_done, n + 1)
                    for t in range(NT):
                        ins = dve.tensor_scalar(tok[:, t, task.i * HD:(task.i + 1) * HD], pv[:, 0, t * HD:(t + 1) * HD],
                                                rden[:, t:t + 1], None, ALU.mult)
                    ins.then_inc(o_done, 1)
                else:
                    hd, t = task.i // 2, task.i % 2
                    dve.tensor_copy(tok[:, t, hd * CV:(hd + 1) * CV], pv[:, 0, 0:CV]).then_inc(o_done, 1)

            def heads_mean(g):
                dve.wait_ge(sub_sq, HEADS_OF_GROUP * (g + 1))
                if g:
                    dve.wait_ge(sub_rstd, g)
                dve.tensor_scalar(sub_var, sub_ss, 1.0 / CV, EPS, ALU.mult, ALU.add).then_inc(sub_var_done, 1)

            def heads_scale(g):
                dve.wait_ge(sub_rstd, g + 1)
                for i in range(HEADS_OF_GROUP):
                    o = tok[:, i % 2, i // 2 * CV:(i // 2 + 1) * CV]
                    ins = dve.scalar_tensor_tensor(o, o, sub_r[:, i:i + 1], sub_gain[:, :], ALU.mult, ALU.mult)
                ins.then_inc(heads_done, 1)

            def decay(i):
                r, a, t = [buf[i % 2] for buf in (rg_r, rg_a, rg_t)]
                dve.wait_ge(rg_act, RG_ACT * (i + 1))
                dve.tensor_tensor(r[:, :, :], a[:, :, :], a[:, :, :], ALU.mult).then_inc(rg_decay, 1)
                dve.wait_ge(rg_decay, RG_DECAY * i + 1)
                dve.scalar_tensor_tensor(t[:, :, :], r[:, :, :], 1.0, t[:, :, :], ALU.add, ALU.mult).then_inc(rg_decay, 1)

            def scan(i):
                k = RG_SCAN * i
                gate_i, a, t = [buf[i % 2] for buf in (rg_i, rg_a, rg_t)]
                for d in range(2):
                    dve.scalar_tensor_tensor(gate_i[:, d, :], gate_i[:, d, :], 1.0, rg_x[i % 2], ALU.add, ALU.mult).then_inc(rg_scan, 1)
                dve.wait_ge(rg_scan, k + 2)
                dve.wait_ge(rg_root_done, i + 1)
                dve.scalar_tensor_tensor(gate_i[:, :, :], gate_i[:, :, :], 0.5, t[:, :, :], ALU.mult, ALU.mult).then_inc(rg_scan, 1)
                dve.wait_ge(rg_scan, k + 3)
                if i:
                    dve.wait_ge(rg_sum, i)
                dve.tensor_tensor_scan(rg_h[:, 0, :], a[:, 0, :], gate_i[:, 0, :], 0.0, ALU.mult, ALU.add).then_inc(rg_scan, 1)
                dve.tensor_tensor_scan(rg_h[:, 1, ::-1], a[:, 1, ::-1], gate_i[:, 1, ::-1], 0.0, ALU.mult, ALU.add).then_inc(rg_scan, 1)

            def recurrence_lo(i):
                r = rg_r[i % 2]
                dve.wait_ge(rg_scan, RG_SCAN * (i + 1))
                dve.tensor_tensor(r[:, 0, :], rg_h[:, 0, :], rg_h[:, 1, :], ALU.add).then_inc(rg_sum, 1)
                dve.wait_ge(rg_sum, i + 1)
                dve.tensor_tensor(r[:, 1, :], r[:, 0, :], geluT[:, i, :], ALU.mult).then_inc(rg_out, 1)
                dve.wait_ge(rg_hi, i + 1)
                dve.tensor_tensor(y_lo[:, i, :], r[:, 1, :], y_hi[:, i, :].bitcast(F32), ALU.subtract).then_inc(rg_out, 1)

            def task_of(task):
                if task.kind == "T":
                    if task.src in ("x", "tok"):
                        operand_lo(task.e, task.m, *region_of(task))
                elif task.kind == "update":
                    update(task)
                elif task.kind in ("rms_x", "rms_y"):
                    mean(task)
                elif task.kind == "lo":
                    if task.u:
                        lo(task.u)
                    else:
                        dve.wait_ge(hi_done, 1)
                        lo_first(slice(KT // 2, KT))
                elif task.kind == "first_half":
                    dve.wait_ge(first_hi, 1)
                    lo_first(slice(0, KT // 2))
                elif task.kind == "add_output":
                    slot = task.slot
                    if slot.w == "ev_out" and slot.starts:
                        dve.wait_ge(rg_out, RG_OUT * AT)
                    add_output(slot.n, slot.u, slot.cb, slot.starts, task.t)
                elif task.kind == "difference":
                    difference(task)
                elif task.kind == "heads_scale":
                    heads_scale(task.g)
                elif task.kind == "gate_up":
                    gate_up(task.n, task.n + 1, task.u, lambda t: dve.wait_ge(tp_done, task.tok_free[t] + 1))
                elif task.kind == "s":
                    softmax(task)
                elif task.kind == "heads":
                    heads_mean(task.g)
                elif task.kind == "pv":
                    values(task)
                elif task.kind == "rg_gates":
                    decay(task.i)
                elif task.kind == "rg_scan":
                    scan(task.i)
                elif task.kind == "rg_out":
                    recurrence_lo(task.i)
                elif task.kind == "par":
                    parameters(task.i)

            v = [0]

            def prep(ins):
                ins.then_inc(prep_v, 1)
                v[0] += 1
                dve.wait_ge(prep_v, v[0])

            def parameters(i):
                lam = par[:, C_LAM:C_LAM + 2 * AT]
                e, s, z, q = poly[:, 0, :], poly[:, 1, :], poly[:, 2, :], poly[:, 3, :]
                if i == 0:
                    dve.wait_ge(par_sb, 1)
                    dve.wait_ge(par_in, 16 * 12)
                    prep(dve.scalar_tensor_tensor(s, lam, -1.0, lam, ALU.mult, ALU.max))
                    for j in range(2):
                        prep(dve.tensor_tensor_reduce(prob[:, j, 0:HD], lqk[:, 2 * HD * j:2 * HD * j + HD],
                                                      lqk[:, 2 * HD * j + HD:2 * HD * (j + 1)], 1.0, 0.0, ALU.mult, ALU.add,
                                                      lam_s[:, j:j + 1]))
                    prep(dve.tensor_scalar(sub_gain[:, :], sub_gain[:, :], 1.0 - LAM_INIT, None, ALU.mult))
                elif i == 2:
                    dve.wait_ge(prep_a, 1)
                    prep(dve.tensor_scalar(s, e, 2.0, None, ALU.add))
                    prep(dve.reciprocal(z, s))
                    prep(dve.tensor_tensor(s, e, z, ALU.mult))
                    prep(dve.tensor_tensor(z, s, s, ALU.mult))
                    prep(dve.tensor_scalar(q, z, 1.0 / (2 * SERIES + 1), None, ALU.mult))
                    for k in range(SERIES - 1, 0, -1):
                        prep(dve.scalar_tensor_tensor(q, q, 1.0 / (2 * k + 1), z, ALU.add, ALU.mult))
                elif i == 3:
                    prep(dve.scalar_tensor_tensor(q, q, 1.0, s, ALU.add, ALU.mult))
                    prep(dve.tensor_scalar(z, lam, -1.0, 0.0, ALU.mult, ALU.max))
                    prep(dve.scalar_tensor_tensor(z, q, 2.0, z, ALU.mult, ALU.add))
                    prep(dve.tensor_scalar(hc[:, 0, :], z, 4.0, None, ALU.mult))
                    prep(dve.tensor_scalar(hc[:, 1, :], z, -4.0, None, ALU.mult))
                    prep(dve.tensor_scalar(par[:, C_BR:C_CW], par[:, C_BR:C_CW], 0.5, None, ALU.mult))
                    dve.wait_ge(prep_a, 2)
                    prep(dve.tensor_tensor(nlam, lam_e[:, 1:2], lam_e[:, 0:1], ALU.subtract))
                    prep(dve.tensor_scalar(nlam, nlam, LAM_INIT, None, ALU.subtract))

            def gate_up(n_gate, n_up, u, tok_free, it=0):
                for t in range(NT):
                    wait_product(dve, u, t, 12 * it)
                    dve.wait_ge(acc_free[n_gate % 2][t], n_gate // 2 + 1 + 3 * it)
                    tok_free(t)
                    dve.scalar_tensor_tensor(tok[:, t, :], acc[n_up % 2][t][:, :], rstd_x[:, t:t + 1], stage[:, t, :],
                                             ALU.mult, ALU.mult).then_inc(acc_free[n_up % 2][t], 1)

            def block_lo(base, it=0):
                for t in range(NT):
                    operand_lo(base.e + t, base.m + t, y_hi[:, 0:KT, t * P:(t + 1) * P],
                               y_lo[:, 0:KT, t * P:(t + 1) * P], it)

            def body(base, start, it=0):
                block_lo(base, it)
                for i in range(12):
                    lo(base.u + i + LO_LEAD, it)
                    if i == 2 * NC - 1:
                        gate_up(base.n, base.n + 1, base.u + i, lambda t: dve.wait_ge(tp_done, base.e + t + 1 + NT * it), it)
                    if i >= 2 * NC:
                        for t in range(NT):
                            add_output(base.n + 2 + i - 2 * NC, base.u + i, i - 2 * NC, start, t, it)

            for part in plan.parts:
                if part.tasks:
                    for task in part.tasks:
                        task_of(task)
                    continue
                body(part.peeled, True)
                with dve.Fori(0, NF - 2) as it:
                    body(part.loop, False, it)
                block_lo(part.tail)

        @block.gpsimd
        def _(pool):
            pool.memset(minus_half, -0.5).then_inc(zero_done, 1)
            pool.wait_ge(zero_done, 1)

            def rsqrt(task):
                pool.wait_ge(var_done, task.stat + 1)
                dst, var = (rstd_x, var_x) if task.kind == "rms_x" else \
                    (rstd_y[:, task.t:task.t + 1], var_y[:, task.t:task.t + 1])
                pool.tensor_tensor(dst, var, minus_half[:, 0:dst.shape[-1]], ALU.pow).then_inc(rstd_done, 1)

            def y_gain(task):
                pool.wait_ge(sq_done, task.sq)
                pool.wait_ge(gain_in[0], 16 * task.b)
                cols = slice(task.c * KC, (task.c + 1) * KC)
                y = yacc[:, task.t, cols]
                pool.tensor_tensor(y, y, post_gain[:, cols], ALU.mult).then_inc(yg_done, 1)

            def gained(task):
                if task.b == 4:
                    return
                if task.b == 0:
                    pool.wait_ge(x_in[task.c], 32)
                else:
                    pool.wait_ge(upd_done, task.update + 1)
                    pool.wait_ge(gain_in[1], 16 * task.b)
                last = (task.stage_free if task.c % 2 else task.tok_free)[task.t]
                if last is not None:
                    pool.wait_ge(tp_done, last + 1)
                cols = slice(task.c * KC, (task.c + 1) * KC)
                pool.tensor_tensor(x_buffer(task.c)[:, task.t, :], xs[:, task.t, cols], pre_gain[:, cols], ALU.mult).then_inc(xg_done, 1)

            def rotate(task):
                for t in range(NT):
                    k = 3 * (task.rope + t)
                    wait_acc(pool, task.n, t)
                    if task.rope + t:
                        pool.wait_ge(rope_done, task.rope + t)
                    else:
                        pool.wait_ge(par_in, 16 * 12)
                        pool.wait_ge(prep_v, 3)
                    heads = stage[:, t, :].rearrange("p (h e) -> p h e", e=HD)
                    h2 = ROT // 2
                    table = ropes[:, t, :].rearrange("p (o e) -> p o e", o=1)

                    def per_head(a, b):
                        return table[:, :, a:b].broadcast_to([P, KC // HD, b - a])
                    pool.tensor_tensor(rot[:, 0], heads[:, :, 0:ROT], per_head(0, ROT), ALU.mult).then_inc(rope_part, 1)
                    pool.tensor_tensor(rot[:, 1, :, 0:h2], heads[:, :, h2:ROT], per_head(ROT, ROT + h2), ALU.mult).then_inc(rope_part, 1)
                    pool.tensor_tensor(rot[:, 1, :, h2:ROT], heads[:, :, 0:h2], per_head(ROT + h2, 2 * ROT), ALU.mult).then_inc(rope_part, 1)
                    pool.wait_ge(rope_part, k + 3)
                    pool.tensor_tensor(heads[:, :, 0:ROT], rot[:, 0], rot[:, 1], ALU.add).then_inc(rope_done, 1)

            def convolve(i):
                k = (2 * CONV - 2) * i
                if i == 0:
                    pool.wait_ge(zero_done, 5)
                    pool.wait_ge(par_sb, 1)
                    pool.wait_ge(prep_v, 3)
                else:
                    pool.wait_ge(conv_done, i)
                for t in range(NT):
                    wait_event(pool, plan.ready["xr", 0, i // KT, t])
                if i >= 2:
                    pool.wait_ge(rg_scan, RG_SCAN * (i - 2) + 2)
                tmp, x_i = prob[:, 1, :], rg_x[i % 2]

                def tap(j, dst):
                    col = C_CW + AT * j + i
                    args = (par[:, col:col + 1], par[:, C_CB + i:C_CB + i + 1], ALU.mult, ALU.add) if j == 0 else \
                        (par[:, col:col + 1], None, ALU.mult)
                    pool.tensor_scalar(dst, xrT[:, i, j:j + T], *args).then_inc(conv_part, 1)
                tap(0, x_i)
                for j in range(1, CONV):
                    tap(j, tmp)
                    pool.wait_ge(conv_part, k + 2 * j)
                    pool.tensor_tensor(x_i, x_i, tmp, ALU.add).then_inc(conv_done if j == CONV - 1 else conv_part, 1)
                    if j < CONV - 1:
                        pool.wait_ge(conv_part, k + 2 * j + 1)

            def task_of(task):
                if task.kind == "update":
                    gained(task)
                elif task.kind == "y_gain":
                    y_gain(task)
                elif task.kind in ("rms_x", "rms_y"):
                    rsqrt(task)
                elif task.kind == "evac" and task.what in ("q", "k"):
                    rotate(task)
                elif task.kind == "rg_conv":
                    convolve(task.i)
                elif task.kind == "heads":
                    pool.wait_ge(sub_var_done, task.g + 1)
                    pool.tensor_tensor(sub_r, sub_var, minus_half, ALU.pow).then_inc(sub_rstd, 1)
                if task.kind == "update" and task.b == 0 and task.c == NC - 1 and task.t == NT - 1:
                    for i in range(2):
                        pool.memset(rg_w[i], 0.0).then_inc(zero_done, 1)
                    pool.wait_ge(xg_done, 8)
                    pool.memset(xrT[:, :, 0:CONV // 2], 0.0).then_inc(zero_done, 1)
                    pool.memset(xrT[:, :, CONV // 2 + T:XP], 0.0).then_inc(zero_done, 1)

            for part in plan.parts:
                for task in part.tasks or ():
                    task_of(task)


def log_counts():
    pairs = ((128, 1), (512, 4), (2048, 16))
    t, k = np.meshgrid(np.arange(T), np.arange(T), indexing="ij")
    count = sum(((t - k) % d == 0) & (abs(t - k) <= w // 2) for w, d in pairs)
    return np.where(count > 0, np.log(np.maximum(count, 1)) / SCALE, NEG).astype(np.float32)


def rope_tables():
    inv = np.float32(500000.0) ** (-np.arange(0, ROT, 2, dtype=np.float32) / np.float32(ROT))
    angle = (np.arange(T, dtype=np.float32)[:, None] * inv[None, :]).astype(np.float32)
    cos, sin = np.cos(angle), np.sin(angle)
    return np.concatenate([cos, cos, -sin, sin], axis=1).astype(np.float32)


_INS = ["x", "norm_mix_pre", "norm_mix_post", "norm_ffn_pre", "norm_ffn_post", "ev_w_in", "ev_conv_w", "ev_conv_b",
        "ev_w_r", "ev_b_r", "ev_w_i", "ev_b_i", "ev_lam", "ev_w_out", "od_w_in", "od_lam_q1", "od_lam_k1",
        "od_lam_q2", "od_lam_k2", "od_subln", "od_w_out", "ffn_w_gate", "ffn_w_up", "ffn_w_down"]


def kernel(**inputs):
    import concourse.bacc as bacc
    from concourse.bass_utils import run_bass_kernel_spmd

    nc = bacc.Bacc("TRN2", target_bir_lowering=False, num_devices=1, dynamic_dma_scratch_size=SCRATCH)
    arrays = {name: np.ascontiguousarray(inputs[name]) for name in _INS}
    arrays["log_count"] = log_counts()
    arrays["rope"] = rope_tables()
    arrays["identity"] = np.eye(P, dtype=np.float32)
    args = [nc.dram_tensor(f"in_{n}", a.shape, mybir.dt.from_np(a.dtype), kind="ExternalInput").ap()
            for n, a in arrays.items()]
    args.append(nc.dram_tensor("out_0", arrays["x"].shape, F32, kind="ExternalOutput").ap())
    trunk(nc, *args)
    result = run_bass_kernel_spmd(nc, [{f"in_{n}": a for n, a in arrays.items()}], core_ids=[0])
    return result.results[0]["out_0"]
```
